# Optimizing a Trainium2 kernel written in Bass

```python
import jax, jax.numpy as jnp
from jax import lax
import numpy as np

D_MODEL = 1024
BATCH = 1
SEQ = 512
DEPTH = 1

PLE_DIM = 256
HEAD_DIM = 64
MOBA_HEADS = 8
MOBA_BLOCK = 256
MOBA_TOPK = 3
MOBA_Q_CHUNK = 16
DIFF_HEADS = 4
DIFF_V_DIM = 2 * HEAD_DIM
ROPE_THETA = 500000.0
ROPE_DIM = HEAD_DIM // 4
DENSE_Q_BLOCK = 128
EPS = 1e-6
MOBA_W = MOBA_HEADS * HEAD_DIM
DIFF_QK_W = DIFF_HEADS * 2 * HEAD_DIM
DIFF_W = DIFF_HEADS * DIFF_V_DIM
MIX_W = MOBA_W + DIFF_W
SPLIT_SIZES = (MOBA_W, MOBA_W, MOBA_W, DIFF_QK_W, DIFF_QK_W, DIFF_W, MIX_W)
PROJ_W = sum(SPLIT_SIZES)

kernel_name = "hybrid_moba_diffattn_gated_ple"

def rmsnorm(x, g):
    xf = x.astype(jnp.float32)
    xf = xf * lax.rsqrt(jnp.mean(xf * xf, axis=-1, keepdims=True) + EPS)
    return (xf * g.astype(jnp.float32)).astype(x.dtype)

def rope_tables(seq):
    inv = ROPE_THETA ** (-jnp.arange(0, ROPE_DIM, 2, dtype=jnp.float32) / ROPE_DIM)
    ang = jnp.arange(seq, dtype=jnp.float32)[:, None] * inv[None, :]
    return jnp.cos(ang), jnp.sin(ang)

def partial_rope(x, cos, sin):
    half = ROPE_DIM // 2
    x1, x2, rest = x[..., :half], x[..., half:ROPE_DIM], x[..., ROPE_DIM:]
    c, s = cos.astype(x.dtype), sin.astype(x.dtype)
    return jnp.concatenate([x1 * c - x2 * s, x2 * c + x1 * s, rest], axis=-1)

def moba_attention(q, k, v, cos, sin):
    B, H, S, dh = q.shape
    q = partial_rope(q, cos, sin)
    k = partial_rope(k, cos, sin)
    nb = -(-S // MOBA_BLOCK)
    pad = nb * MOBA_BLOCK - S
    kp = jnp.pad(k, ((0, 0), (0, 0), (0, pad), (0, 0)))
    vp = jnp.pad(v, ((0, 0), (0, 0), (0, pad), (0, 0)))
    kb = kp.reshape(B, H, nb, MOBA_BLOCK, dh)
    vb = vp.reshape(B, H, nb, MOBA_BLOCK, dh)
    kmean = jnp.mean(kb.astype(jnp.float32), axis=3)
    n_sel = min(MOBA_TOPK, nb)
    scale = dh ** -0.5
    bi = jnp.arange(B)[:, None, None, None]
    hi = jnp.arange(H)[None, :, None, None]
    blk_ids = jnp.arange(nb)
    key_off = jnp.arange(MOBA_BLOCK)

    def chunk(c):
        start = c * MOBA_Q_CHUNK
        qc = lax.dynamic_slice_in_dim(q, start, MOBA_Q_CHUNK, axis=2)
        qpos = start + jnp.arange(MOBA_Q_CHUNK)
        own = start // MOBA_BLOCK
        gate = jnp.einsum('bhqd,bhnd->bhqn', qc.astype(jnp.float32), kmean)
        gate = jnp.where(blk_ids < own, gate, -jnp.inf)
        _, sel = lax.top_k(gate, n_sel)
        sel_ok = sel < own
        ks = kb[bi, hi, sel]
        vs = vb[bi, hi, sel]
        s_sel = jnp.einsum('bhqd,bhqnkd->bhqnk', qc, ks).astype(jnp.float32) * scale
        s_sel = jnp.where(sel_ok[..., None], s_sel, -jnp.inf)
        s_sel = s_sel.reshape(B, H, MOBA_Q_CHUNK, n_sel * MOBA_BLOCK)
        ko = lax.dynamic_slice_in_dim(kp, own * MOBA_BLOCK, MOBA_BLOCK, axis=2)
        vo = lax.dynamic_slice_in_dim(vp, own * MOBA_BLOCK, MOBA_BLOCK, axis=2)
        kpos = own * MOBA_BLOCK + key_off
        s_own = jnp.einsum('bhqd,bhkd->bhqk', qc, ko).astype(jnp.float32) * scale
        s_own = jnp.where(kpos[None, :] <= qpos[:, None], s_own, -jnp.inf)
        probs = jax.nn.softmax(jnp.concatenate([s_sel, s_own], axis=-1), axis=-1).astype(v.dtype)
        p_sel = probs[..., :n_sel * MOBA_BLOCK].reshape(B, H, MOBA_Q_CHUNK, n_sel, MOBA_BLOCK)
        p_own = probs[..., n_sel * MOBA_BLOCK:]
        return (jnp.einsum('bhqnk,bhqnkd->bhqd', p_sel, vs)
                + jnp.einsum('bhqk,bhkd->bhqd', p_own, vo))

    outs = lax.map(chunk, jnp.arange(S // MOBA_Q_CHUNK))
    return outs.transpose(1, 2, 0, 3, 4).reshape(B, H, S, dh)

def diff_attention(q, k, v, lam, g_subln, lambda_init, cos, sin):
    B, H, _, S, dh = q.shape
    q = partial_rope(q, cos, sin)
    k = partial_rope(k, cos, sin)
    scale = dh ** -0.5
    kpos = jnp.arange(S)

    def block(c):
        start = c * DENSE_Q_BLOCK
        qc = lax.dynamic_slice_in_dim(q, start, DENSE_Q_BLOCK, axis=3)
        s = jnp.einsum('bhiqd,bhikd->bhiqk', qc, k).astype(jnp.float32) * scale
        qpos = start + jnp.arange(DENSE_Q_BLOCK)
        s = jnp.where(kpos[None, :] <= qpos[:, None], s, -jnp.inf)
        pr = jax.nn.softmax(s, axis=-1)
        a = pr[:, :, 0] - lam * pr[:, :, 1]
        return jnp.einsum('bhqk,bhkd->bhqd', a.astype(v.dtype), v)

    o = lax.map(block, jnp.arange(S // DENSE_Q_BLOCK))
    o = o.transpose(1, 2, 0, 3, 4).reshape(B, H, S, 2 * dh)
    return rmsnorm(o, g_subln) * (1.0 - lambda_init)

def setup_inputs(seed: int = 0) -> dict:
    key = jax.random.key(seed)
    ks = jax.random.split(key, 14)
    f32 = jnp.float32
    nrm = lambda k, shape, s: jax.random.normal(k, shape, f32) * s
    return {
        "x": nrm(ks[0], (BATCH, SEQ, D_MODEL), 1.0),
        "p": nrm(ks[1], (DEPTH, BATCH, SEQ, PLE_DIM), 1.0),
        "w_in": nrm(ks[2], (DEPTH, D_MODEL, PROJ_W), D_MODEL ** -0.5),
        "w_out": nrm(ks[3], (DEPTH, MIX_W, D_MODEL), MIX_W ** -0.5),
        "g_mix": 1.0 + nrm(ks[4], (DEPTH, D_MODEL), 0.02),
        "diff_lq1": nrm(ks[5], (DEPTH, HEAD_DIM), 0.1),
        "diff_lk1": nrm(ks[6], (DEPTH, HEAD_DIM), 0.1),
        "diff_lq2": nrm(ks[7], (DEPTH, HEAD_DIM), 0.1),
        "diff_lk2": nrm(ks[8], (DEPTH, HEAD_DIM), 0.1),
        "g_subln": 1.0 + nrm(ks[9], (DEPTH, DIFF_V_DIM), 0.02),
        "w_ple": nrm(ks[10], (DEPTH, PLE_DIM, D_MODEL), PLE_DIM ** -0.5),
        "w_ple_gate": nrm(ks[11], (DEPTH, D_MODEL, D_MODEL), D_MODEL ** -0.5),
        "g_ple": 1.0 + nrm(ks[12], (DEPTH, D_MODEL), 0.02),
        "g_final": 1.0 + nrm(ks[13], (D_MODEL,), 0.02),
    }

def reference(x, p, w_in, w_out, g_mix, diff_lq1, diff_lk1, diff_lq2, diff_lk2,
              g_subln, w_ple, w_ple_gate, g_ple, g_final):
    B, S, _ = x.shape
    cos, sin = rope_tables(S)
    offsets = [int(o) for o in np.cumsum(SPLIT_SIZES)[:-1]]
    h = x
    for i in range(DEPTH):
        lambda_init = 0.8 - 0.6 * float(np.exp(-0.3 * i))
        u = rmsnorm(h, g_mix[i])
        proj = jnp.einsum('bsd,de->bse', u, w_in[i])
        mq, mk, mv, dq, dk, dv, z = jnp.split(proj, offsets, axis=-1)
        to_heads = lambda t: t.reshape(B, S, MOBA_HEADS, HEAD_DIM).transpose(0, 2, 1, 3)
        m_out = moba_attention(to_heads(mq), to_heads(mk), to_heads(mv), cos, sin)
        m_out = m_out.transpose(0, 2, 1, 3).reshape(B, S, MOBA_W)
        dq = dq.reshape(B, S, DIFF_HEADS, 2, HEAD_DIM).transpose(0, 2, 3, 1, 4)
        dk = dk.reshape(B, S, DIFF_HEADS, 2, HEAD_DIM).transpose(0, 2, 3, 1, 4)
        dv = dv.reshape(B, S, DIFF_HEADS, DIFF_V_DIM).transpose(0, 2, 1, 3)
        lam = (jnp.exp(jnp.sum(diff_lq1[i].astype(jnp.float32) * diff_lk1[i].astype(jnp.float32)))
               - jnp.exp(jnp.sum(diff_lq2[i].astype(jnp.float32) * diff_lk2[i].astype(jnp.float32)))
               + lambda_init)
        d_out = diff_attention(dq, dk, dv, lam, g_subln[i], lambda_init, cos, sin)
        d_out = d_out.transpose(0, 2, 1, 3).reshape(B, S, DIFF_W)
        y = jnp.concatenate([m_out, d_out], axis=-1) * jax.nn.silu(z)
        h = h + jnp.einsum('bse,ed->bsd', y, w_out[i])
        pe = jnp.einsum('bsk,kd->bsd', p[i], w_ple[i])
        gate = jax.nn.sigmoid(jnp.einsum('bsd,de->bse', rmsnorm(h, g_ple[i]), w_ple_gate[i]))
        h = h + gate * pe
    return rmsnorm(h, g_final)


_drawn_inputs = setup_inputs


def setup_inputs(seed=0):
    import zlib

    import numpy as np

    out = dict(_drawn_inputs(seed))
    spreads = {}
    factors = {'g_mix': 4.607,
     'diff_lq1': 200.0,
     'diff_lq2': 3.226,
     'diff_lk2': 4.96,
     'g_subln': 24.585,
     'g_ple': 200.0,
     'g_final': 20.62,
     'p': 3.633,
     'w_ple': 3.626,
     'w_ple_gate': 5.163}
    for name, (base, spread) in spreads.items():
        noise = np.random.default_rng([zlib.crc32(name.encode()), seed]).standard_normal(out[name].shape)
        drawn = base * np.exp(spread * noise) if base else spread * noise
        out[name] = __import__('jax').numpy.asarray(drawn.astype(out[name].dtype))
    for name, factor in factors.items():
        out[name] = (out[name] * factor).astype(out[name].dtype)
    return out
```

```python
import numpy as np
import concourse.bass as bass
from concourse import mybir
from concourse.alu_op_type import AluOpType as ALU
from contextlib import ExitStack

D_MODEL, SEQ, PLE_DIM, HEAD_DIM = 1024, 512, 256, 64
MOBA_HEADS, MOBA_BLOCK, MOBA_TOPK, DIFF_HEADS = 8, 256, 3, 4
ROPE_THETA, ROPE_DIM = 500000.0, 16
EPS = 1e-6
LAMBDA_INIT = 0.8 - 0.6 * 1.0
P = 128
assert min(MOBA_TOPK, SEQ // MOBA_BLOCK) == SEQ // MOBA_BLOCK


def build_program(nc, x_t, x, p_t, w_in, w_out, w_gate, w_ple, g_mix, g_ple, g_subln, g_final, lams,
                  rope, consts, out):
    f32, f32r = mybir.dt.float32, mybir.dt.float32r
    ACT = mybir.ActivationFunctionType
    AX = mybir.AxisListType

    KT = D_MODEL // P
    ST = SEQ // P
    NU = D_MODEL // P
    MOBA_UNITS = MOBA_HEADS * HEAD_DIM // P
    NH = D_MODEL // SEQ
    HALF = HEAD_DIM
    Q, K, Z, V = range(4)
    STEPS = 3
    STEP_TILES = [(0, 1), (2,), (3,)]
    STEP_COL = [0, 384, 768]
    STEP_W = [384, 384, 512]
    PT_BLOCKS = 12
    SCALE = float(HEAD_DIM) ** -0.5

    T_IN = 0
    T_PLE = T_IN + 4 * NU
    T_P = T_PLE + 2
    T_OUT = T_P + 1
    T_GATE = T_OUT + NH * KT // 2
    T_ALL = T_GATE + NH * KT // 2
    RAW = 4

    ctx = ExitStack()
    with ctx:
        def sb(name, shape, dt=f32):
            return ctx.enter_context(nc.sbuf_tensor(name, shape, dt))

        def sem(name):
            return ctx.enter_context(nc.semaphore(name))

        wsplit = sb("wsplit", [P, 4, 2, 1024], f32r)
        usplit = sb("usplit", [P, 2, KT, SEQ], f32r)
        csplit = sb("csplit", [P, 9216], f32r)
        ysplit = sb("ysplit", [P, 2, NU, SEQ], f32r)
        vsplit = sb("vsplit", [P, ST, 2 * P], f32r)
        pt_hi = csplit[:, 0:3072].rearrange("p (m c) -> p m c", m=2)
        pt_lo = csplit[:, 3072:6144].rearrange("p (m c) -> p m c", m=2)
        qs = csplit[:, 6144:7168].rearrange("p (m c) -> p m c", m=2)
        k_hi = csplit[:, 7168:8192].rearrange("p (m c) -> p m c", m=2)
        k_lo = csplit[:, 8192:9216].rearrange("p (m c) -> p m c", m=2)
        wout_n = [usplit[:, :, :, :].rearrange("p s k c -> p (s k c)"),
                  wsplit[:, :, :, :].rearrange("p a s c -> p (a s c)")]
        wgate_n = [csplit[:, 0:8192], wsplit[:, :, :, :].rearrange("p a s c -> p (a s c)")]

        def chunk(region, c):
            v = region.rearrange("p (c s n) -> p c s n", c=KT // 2, s=2)
            return v[:, c, 0, :], v[:, c, 1, :]

        def chunk_tile(region, kt):
            hi, lo = chunk(region, kt // 2)
            o = (kt % 2) * SEQ
            return hi[:, o:o + SEQ], lo[:, o:o + SEQ]

        raw = sb("raw", [P, RAW, 1024])
        hbuf = sb("hbuf", [P, 4096])
        tbuf = sb("tbuf", [P, 4096])
        xt_raw = hbuf[:, :].rearrange("p (k c) -> p k c", k=KT)
        probs = hbuf[:, 0:2560].rearrange("p (m c) -> p m c", m=2)
        zbuf = hbuf[:, 2560:4096].rearrange("p (b c) -> p b c", b=3)
        h = hbuf[:, :].rearrange("p (s d) -> p s d", s=ST)
        shuf = tbuf[:, 0:1024].rearrange("p (b c) -> p b c", b=2)
        rot = tbuf[:, 1024:2048].rearrange("p (b c) -> p b c", b=2)
        rope_r = tbuf[:, 2048:3072].rearrange("p (b c) -> p b c", b=2)
        rstd = tbuf[:, 3072:3584]
        ztanh = tbuf[:, 3584:4096]
        pe = tbuf[:, :].rearrange("p (s d) -> p s d", s=ST)
        v_t = sb("v_t", [P, SEQ])
        o_sb = sb("o_sb", [P, SEQ])
        o_tmp = sb("o_tmp", [P, SEQ])
        sq = sb("sq", [P, 2, SEQ])
        gfin = sb("gfin", [P, D_MODEL])
        cst = sb("cst", [P, 3 * P])
        ident, mask, ones = cst[:, 0:P], cst[:, P:2 * P], cst[:, 2 * P:3 * P]
        gm = sb("gm", [P, KT])
        gp = sb("gp", [P, KT])
        gs = sb("gs", [P, 1])
        gs8 = sb("gs8", [P, 1])
        lam_in = sb("lam_in", [P, 4, HEAD_DIM])
        lam_pr = sb("lam_pr", [P, 2, HEAD_DIM])
        lam_s = sb("lam_s", [P, 2])
        lam_e = sb("lam_e", [P, 2])
        nlam = sb("nlam", [P, 1])
        eps = sb("eps", [P, 1])
        mhalf = sb("mhalf", [P, ST])
        nmax = sb("nmax", [P, ST, 2])
        rsum = sb("rsum", [P, ST, 2])
        rinv = sb("rinv", [P, ST, 2])
        ssq = sb("ssq", [P, ST, 2])
        ssa = sb("ssa", [P, ST])
        hrs = sb("hrs", [P, ST])
        fsq = sb("fsq", [P, ST, 2])
        fsa = sb("fsa", [P, ST])
        frs = sb("frs", [P, ST])

        def ps(name):
            return ctx.enter_context(nc.psum_tensor(name, [P, 2, SEQ], f32))

        pj, sc, tr, ou = ps("pj"), ps("sc"), ps("tr"), ps("ou")
        banks = [pj[:, 0, :], pj[:, 1, :], sc[:, 0, :], sc[:, 1, :],
                 tr[:, 0, :], tr[:, 1, :], ou[:, 0, :], ou[:, 1, :]]

        raw_in = [sem(f"raw_in{i}") for i in range(RAW)]
        xt_in = [sem(f"xt_in{k}") for k in range(KT)]
        x_in = [sem(f"x_in{t}") for t in range(ST)]
        gm_in, small_in, cst_in, rope_in, stored = [sem(n) for n in "gm_in small_in cst_in rope_in stored".split()]
        u_hi, u_lo, x_sq, x_sum, x_ms, x_std, x_rstd, tab_done = [
            sem(n) for n in "u_hi u_lo x_sq x_sum x_ms x_std x_rstd tab_done".split()]
        lam_prod, lam_sum, lam_exp, lam_done, gs_done, set_done = [
            sem(n) for n in "lam_prod lam_sum lam_exp lam_done gs_done set_done".split()]
        w_hi, w_lo, proj, pj_read, turned, roped, qk_hi, qk_lo = [
            sem(n) for n in "w_hi w_lo proj pj_read turned roped qk_hi qk_lo".split()]
        scores, masked, maxes, exps, recips, weighted, probs_ready, ptrans, p_hi, p_lo = [
            sem(n) for n in "scores masked maxes exps recips weighted probs_ready ptrans p_hi p_lo".split()]
        vtrans, v_hi, v_lo, pv, o_half, o_read, o_sq, o_ms, o_std, o_inv, o_norm = [
            sem(n) for n in "vtrans v_hi v_lo pv o_half o_read o_sq o_ms o_std o_inv o_norm".split()]
        z_tanh, z_done, y_ready, y_hi, y_lo = [sem(n) for n in "z_tanh z_done y_ready y_hi y_lo".split()]
        pe_mm, pe_read, item, h_read, h_sq, h_rstd, ht_hi, ht_lo = [
            sem(n) for n in "pe_mm pe_read item h_read h_sq h_rstd ht_hi ht_lo".split()]
        g_tanh, g_mul, g_add, f_sq, f_rstd, f_out, pool_own = [
            sem(n) for n in "g_tanh g_mul g_add f_sq f_rstd f_out pool_own".split()]

        def split_target(j):
            if j < T_OUT:
                return wsplit[:, j % 4, 0, :], wsplit[:, j % 4, 1, :]
            t, region = (j - T_OUT, wout_n) if j < T_GATE else (j - T_GATE, wgate_n)
            return chunk(region[t // (KT // 2)], t % (KT // 2))

        def raw_ready(eng, j):
            eng.wait_ge(raw_in[j % RAW], 16 * (j // RAW + 1))

        def pt_blocks(step):
            return [[(0, 0, 1, 2), (2, 5, 1, 1)], [(0, 2, 4, 3)], [(0, 3, 4, 3), (3, 8, 1, 1)]][step]

        def pt_views(store, step):
            for first, to, stride, n in pt_blocks(step):
                src = tr[:, :, first * P:(first + n) * P].rearrange("p m (b c) -> p m b c", b=n)
                dst = store.rearrange("p m (b c) -> p m b c", c=P)[:, :, to:to + stride * (n - 1) + 1:stride, :]
                yield src, dst

        def per_map(pairs, moba):
            for src, dst in pairs:
                for m in range(2 if moba else 1):
                    yield src[:, m], dst[:, m]

        ITEMS = ([("out", 0, t) for t in range(ST)] + [("out", 1, 0), ("out", 1, 1), ("out", 1, 2), ("turn", 0, 0), ("turn", 1, 0),
                 ("out", 1, 3), ("turn", 0, 1), ("turn", 1, 1), ("gate", 0, 0), ("turn", 0, 2), ("turn", 1, 2), ("gate", 0, 1),
                 ("turn", 0, 3), ("turn", 1, 3), ("gate", 0, 2), ("gate", 0, 3)] + [("gate", 1, t) for t in range(ST)])
        BANK = list(range(7)) + [(0, 1, 7, 2, 3, 4, 5, 6)[i % 8] for i in range(len(ITEMS) - 7)]

        def nth(i):
            return sum(k[0] == ITEMS[i][0] for k in ITEMS[:i + 1])

        def number(kind, n, t):
            return ITEMS.index((kind, n, t))

        block = ctx.enter_context(nc.Block())

        @block.sync
        def _(sp):
            def load_tile(j):
                if j >= RAW:
                    sp.wait_ge(w_lo, j - RAW + 1)
                dst, halves = raw[:, j % RAW, :], raw[:, j % RAW, :].rearrange("p (k c) -> p k c", k=2)
                if j < T_PLE:
                    src = w_in[j // 4, :, j % 4, :]
                elif j < T_P:
                    src = w_ple[(j - T_PLE) * P:(j - T_PLE + 1) * P, :]
                elif j < T_OUT:
                    dst, src = halves, p_t.rearrange("(k p) c -> p k c", k=2)
                else:
                    w, t = (w_out, j - T_OUT) if j < T_GATE else (w_gate, j - T_GATE)
                    n, c = divmod(t, KT // 2)
                    dst = halves
                    src = w[2 * c * P:(2 * c + 2) * P, n * SEQ:(n + 1) * SEQ].rearrange("(k p) c -> p k c", k=2)
                sp.dma_start(dst, src).then_inc(raw_in[j % RAW], 16)

            for j in range(T_GATE):
                load_tile(j)
            sp.wait_ge(y_ready, NU)
            for t in range(ST):
                sp.dma_start(h[:, t, :], x[t * P:(t + 1) * P, :]).then_inc(x_in[t], 16)
            for j in range(T_GATE, T_ALL):
                load_tile(j)
            for t in range(ST):
                sp.wait_ge(f_out, t + 1)
                sp.dma_start(out[t * P:(t + 1) * P, :], h[:, t, :]).then_inc(stored, 16)
            sp.wait_ge(stored, 16 * ST)

        @block.tensor
        def _(pe_eng):
            mm = nc.tensor.matmul

            def project(u, t):
                j = 4 * u + t
                pe_eng.wait_ge(w_lo, j + 1)
                if j >= 2:
                    pe_eng.wait_ge(pj_read, j - 1)
                o = pj[:, j % 2, :]
                for kt in range(KT):
                    if j == 0:
                        pe_eng.wait_ge(u_lo, kt + 1)
                    w_h, w_l = (wsplit[:, j % 4, i, kt * P:(kt + 1) * P] for i in range(2))
                    mm(o, w_h, usplit[:, 0, kt, :], start=kt == 0, stop=False)
                    mm(o, w_h, usplit[:, 1, kt, :], start=False, stop=False)
                    last = mm(o, w_l, usplit[:, 0, kt, :], start=False, stop=kt == KT - 1)
                last.then_inc(proj, 1)

            def score(u, step):
                if step == 0:
                    pe_eng.wait_ge(qk_lo, u + 1)
                if 3 * u + step:
                    pe_eng.wait_ge(exps, 3 * u + step)
                for m in range(2):
                    c = 0
                    for q in STEP_TILES[step]:
                        n = (q + 1) * P
                        o, w = sc[:, m, c:c + n], qs[:, m, q * P:(q + 1) * P]
                        mm(o, w, k_hi[:, m, 0:n], start=True, stop=False)
                        last = mm(o, w, k_lo[:, m, 0:n], start=False, stop=True)
                        c += n
                last.then_inc(scores, 1)

            def turn_probs(u, step):
                n = 3 * u + step
                pe_eng.wait_ge(probs_ready, n + 1)
                if n:
                    pe_eng.wait_ge(p_lo, n)
                for m in range(2 if u < MOBA_UNITS else 1):
                    for b in range(STEP_W[step] // P):
                        c = STEP_COL[step] + b * P
                        last = nc.tensor.transpose(tr[:, m, b * P:(b + 1) * P], probs[:, m, c:c + P], ident)
                last.then_inc(ptrans, 1)

            def turn_values(u):
                pe_eng.wait_ge(pj_read, 4 * u + V + 1)
                if u:
                    if u - 1 < MOBA_UNITS:
                        pe_eng.wait_ge(o_read, u)
                    else:
                        pe_eng.wait_ge(o_half, u)
                for kt in range(ST):
                    last = nc.tensor.transpose(ou[:, 0, kt * P:(kt + 1) * P], v_t[:, kt * P:(kt + 1) * P], ident)
                last.then_inc(vtrans, 1)

            def weigh_values(u):
                pe_eng.wait_ge(v_lo, u + 1)
                pe_eng.wait_ge(p_lo, 3 * u + 3)
                if u:
                    pe_eng.wait_ge(o_read, u)
                moba = u < MOBA_UNITS
                for m in range(2 if moba else 1):
                    for kt in range(ST):
                        b, n = (5 * kt if kt < 3 else 8) * P, (ST - kt) * P
                        o = ou[:, m, kt * P:SEQ]
                        ph, pl = pt_hi[:, m, b:b + n], pt_lo[:, m, b:b + n]
                        first, end = kt == 0, kt == ST - 1
                        if moba:
                            v = vsplit[:, kt, m * P:(m + 1) * P]
                            mm(o, v, ph, start=first, stop=False)
                            last = mm(o, v, pl, start=False, stop=end)
                        else:
                            mm(o, vsplit[:, kt, 0:P], ph, start=first, stop=False)
                            mm(o, vsplit[:, kt, 0:P], pl, start=False, stop=False)
                            last = mm(o, vsplit[:, kt, P:2 * P], ph, start=False, stop=end)
                last.then_inc(pv, 1)

            def square_sum(u):
                pe_eng.wait_ge(o_sq, u - MOBA_UNITS + 1)
                mm(ou[:, 1, :], ones, o_tmp[:, :], start=True, stop=True).then_inc(o_ms, 1)

            def embed(g):
                t, n = divmod(g, NH)
                if g == 0:
                    pe_eng.wait_ge(w_lo, T_OUT)
                if g < 2:
                    pe_eng.wait_ge(pj_read, 4 * NU - 1 + g)
                else:
                    pe_eng.wait_ge(pe_read, g - 1)
                o = pj[:, g % 2, :]
                for kt in range(2):
                    p_h, p_l = (wsplit[:, 2, i, kt * SEQ + t * P:kt * SEQ + (t + 1) * P] for i in range(2))
                    w_h, w_l = (wsplit[:, kt, i, n * SEQ:(n + 1) * SEQ] for i in range(2))
                    mm(o, p_h, w_h, start=kt == 0, stop=False)
                    mm(o, p_h, w_l, start=False, stop=False)
                    last = mm(o, p_l, w_h, start=False, stop=kt == 1)
                last.then_inc(pe_mm, 1)

            def bank_free(i):
                before = [k for k in range(i) if BANK[k] == BANK[i]]
                if before:
                    b = before[-1]
                    pe_eng.wait_ge({"out": h_read, "turn": ht_lo, "gate": g_tanh}[ITEMS[b][0]], nth(b))
                elif BANK[i] < 2:
                    pe_eng.wait_ge(pe_read, ST * NH - 1 + BANK[i])
                elif BANK[i] < 4:
                    pe_eng.wait_ge(exps, STEPS * NU)
                elif BANK[i] < 6:
                    pe_eng.wait_ge(p_lo, STEPS * NU)
                else:
                    pe_eng.wait_ge(o_read, NU)

            def accumulate(i, left, region, kts):
                t = ITEMS[i][2]
                for kt in kts:
                    a_h, a_l = (left[:, k, kt, t * P:(t + 1) * P] for k in range(2))
                    w_h, w_l = chunk_tile(region, kt)
                    mm(banks[BANK[i]], a_h, w_h, start=kt == 0, stop=False)
                    mm(banks[BANK[i]], a_h, w_l, start=False, stop=False)
                    last = mm(banks[BANK[i]], a_l, w_h, start=False, stop=kt == KT - 1)
                if kts[-1] == KT - 1:
                    last.then_inc(item, 1)

            def mix_out(i, kts):
                n = ITEMS[i][1]
                if kts[0] == 0:
                    bank_free(i)
                pe_eng.wait_ge(w_lo, T_OUT + n * KT // 2 + kts[-1] // 2 + 1)
                pe_eng.wait_ge(y_lo, kts[-1] + 1)
                accumulate(i, ysplit, wout_n[n], kts)

            def turn_h(i):
                _, n, t = ITEMS[i]
                bank_free(i)
                pe_eng.wait_ge(h_read, nth(number("out", n, t)))
                for b in range(4):
                    c = n * SEQ + b * P
                    last = nc.tensor.transpose(banks[BANK[i]][:, b * P:(b + 1) * P], h[:, t, c:c + P], ident)
                last.then_inc(item, 1)

            def gate(i):
                _, n, t = ITEMS[i]
                bank_free(i)
                pe_eng.wait_ge(w_lo, T_GATE + (n + 1) * KT // 2)
                pe_eng.wait_ge(ht_lo, nth(number("turn", 1, t)))
                accumulate(i, usplit, wgate_n[n], range(KT))

            for u in range(NU):
                project(u, Q)
                if u >= 2:
                    turn_probs(u - 2, 1)
                project(u, K)
                if u == 0:
                    pe_eng.wait_ge(cst_in, 16)
                    pe_eng.wait_ge(x_sum, KT - 1)
                    mm(ou[:, 1, :], ones, sq[:, 0, :], start=True, stop=True).then_inc(x_ms, 1)
                if u >= 2:
                    turn_probs(u - 2, 2)
                if u >= 1:
                    score(u - 1, 0)
                project(u, Z)
                if u >= 1:
                    score(u - 1, 1)
                if u >= 2:
                    weigh_values(u - 2)
                project(u, V)
                if u >= 1:
                    score(u - 1, 2)
                    turn_probs(u - 1, 0)
                if u - 2 >= MOBA_UNITS:
                    square_sum(u - 2)
                if u >= 1:
                    turn_values(u - 1)
            embed(0), embed(1)
            turn_probs(NU - 2, 1)
            embed(2)
            score(NU - 1, 0)
            embed(3)
            turn_probs(NU - 2, 2)
            embed(4)
            score(NU - 1, 1)
            embed(5)
            weigh_values(NU - 2)
            score(NU - 1, 2)
            turn_probs(NU - 1, 0)
            embed(6), embed(7)
            square_sum(NU - 2)
            turn_values(NU - 1)
            mix_out(0, range(0, 2))
            turn_probs(NU - 1, 1)
            mix_out(0, range(2, 6))
            turn_probs(NU - 1, 2)
            mix_out(1, range(0, 6))
            weigh_values(NU - 1)
            mix_out(2, range(0, 6))
            square_sum(NU - 1)
            mix_out(3, range(0, 6))
            for i in range(4):
                mix_out(i, range(6, 7))
            for i in range(4):
                mix_out(i, range(7, 8))
            for i in range(4, len(ITEMS)):
                if ITEMS[i][0] == "out":
                    mix_out(i, range(KT))
                elif ITEMS[i][0] == "turn":
                    turn_h(i)
                else:
                    gate(i)

        @block.scalar
        def _(act):
            A = nc.scalar.activation

            def weights_hi(j):
                raw_ready(act, j)
                if 4 <= j < T_OUT:
                    act.wait_ge(proj, j - 3)
                elif j >= T_GATE + KT // 2:
                    act.wait_ge(item, 1 + number("out", 1, 3))
                elif j >= T_GATE:
                    act.wait_ge(pv, NU)
                elif j >= T_OUT + KT // 2:
                    act.wait_ge(pe_mm, ST * NH)
                elif j >= T_OUT:
                    act.wait_ge(proj, 4 * NU)
                hi = split_target(j)[0]
                if j < T_GATE:
                    A(hi, raw[:, j % RAW, :], ACT.Copy).then_inc(w_hi, 1)
                else:
                    for k in range(2):
                        kt = 2 * ((j - T_GATE) % (KT // 2)) + k
                        last = A(hi[:, k * SEQ:(k + 1) * SEQ], raw[:, j % RAW, k * SEQ:(k + 1) * SEQ], ACT.Copy, scale=gp[:, kt:kt + 1])
                    last.then_inc(w_hi, 1)

            def exponentials(u, step):
                act.wait_ge(maxes, 3 * u + step + 1)
                if u:
                    act.wait_ge(ptrans, 3 * u + step - 2)
                c = 0
                for q in STEP_TILES[step]:
                    n = (q + 1) * P
                    for m in range(2):
                        last = A(probs[:, m, STEP_COL[step] + c:STEP_COL[step] + c + n], sc[:, m, c:c + n], ACT.Exp,
                                 bias=nmax[:, q, m:m + 1], accum_out=rsum[:, q, m:m + 1])
                    c += n
                last.then_inc(exps, 1)

            def probs_hi(u, step):
                act.wait_ge(ptrans, 3 * u + step + 1)
                if step == 0 and u:
                    act.wait_ge(pv, u)
                for src, dst in per_map(pt_views(pt_hi, step), u < MOBA_UNITS):
                    last = A(dst, src, ACT.Copy)
                last.then_inc(p_hi, 1)

            def qk_stack_hi(u):
                act.wait_ge(roped, 2 * u + 1)
                if u:
                    act.wait_ge(scores, 3 * u)
                A(qs[0:HALF, 0, :], rot[0:HALF, 0, :], ACT.Copy, scale=SCALE)
                A(qs[HALF:P, 1, :], rot[HALF:P, 0, :], ACT.Copy, scale=SCALE)
                act.wait_ge(roped, 2 * u + 2)
                for m in range(2):
                    for half in range(2):
                        last = A(k_hi[half * HALF:(half + 1) * HALF, m, :], rot[m * HALF:(m + 1) * HALF, 1, :], ACT.Copy)
                last.then_inc(qk_hi, 1)

            def values_hi(u):
                act.wait_ge(vtrans, u + 1)
                if u:
                    act.wait_ge(pv, u)
                if u < MOBA_UNITS:
                    dst = vsplit[:, :, :].rearrange("p k (m i d) -> p k m i d", m=2, i=2)[:, :, :, 0, :]
                    src = ou[:, 0, :].rearrange("p (k m d) -> p k m d", k=ST, m=2)
                else:
                    dst = vsplit[:, :, 0:P]
                    src = ou[:, 0, :].rearrange("p (k d) -> p k d", k=ST)
                A(dst, src, ACT.Copy).then_inc(v_hi, 1)

            def output_copy(u):
                act.wait_ge(pv, u + 1)
                if u < MOBA_UNITS:
                    if u:
                        act.wait_ge(o_read, u)
                    A(o_tmp[0:HALF, :], ou[HALF:P, 0, :], ACT.Copy)
                    A(o_tmp[HALF:P, :], ou[0:HALF, 1, :], ACT.Copy).then_inc(o_half, 1)
                else:
                    act.wait_ge(y_lo, u)
                    A(o_sb[:, :], ou[:, 0, :], ACT.Copy).then_inc(o_half, 1)

            def output_std(u):
                act.wait_ge(o_ms, u - MOBA_UNITS + 1)
                A(o_tmp[:, :], ou[:, 1, :], ACT.Sqrt, bias=eps[:, 0:1], scale=1.0 / P).then_inc(o_std, 1)

            def z_gate(u):
                act.wait_ge(pj_read, 4 * u + Z + 1)
                if u:
                    act.wait_ge(z_done, u)
                A(ztanh, zbuf[:, u % 3, :], ACT.Tanh).then_inc(z_tanh, 1)

            def y_round(u):
                act.wait_ge(y_ready, u + 1)
                A(ysplit[:, 0, u, :], o_sb[:, :], ACT.Copy).then_inc(y_hi, 1)

            def embed_read(g):
                t, n = divmod(g, NH)
                act.wait_ge(pe_mm, g + 1)
                if g == 0:
                    act.wait_ge(qk_lo, NU)
                    act.wait_ge(pj_read, 4 * NU)
                A(pe[:, t, n * SEQ:(n + 1) * SEQ], pj[:, g % 2, :], ACT.Copy, scale=0.5).then_inc(pe_read, 1)

            def h_square(k):
                _, n, t = [x for x in ITEMS if x[0] == "out"][k]
                act.wait_ge(h_read, k + 1)
                if k:
                    act.wait_ge(h_sq, k)
                A(sq[:, 1, :], h[:, t, n * SEQ:(n + 1) * SEQ], ACT.Square, accum_out=ssq[:, t, n:n + 1]).then_inc(h_sq, 1)

            def h_turned_hi(k):
                i = [x for x in range(len(ITEMS)) if ITEMS[x][0] == "turn"][k]
                _, n, t = ITEMS[i]
                act.wait_ge(item, i + 1)
                A(usplit[:, 0, 4 * n:4 * n + 4, t * P:(t + 1) * P], banks[BANK[i]].rearrange("p (b c) -> p b c", b=4),
                  ACT.Copy).then_inc(ht_hi, 1)

            def gate_tanh(k):
                i = [x for x in range(len(ITEMS)) if ITEMS[x][0] == "gate"][k]
                t = ITEMS[i][2]
                act.wait_ge(item, i + 1)
                if k == 0:
                    act.wait_ge(h_rstd, 1)
                    act.wait_ge(y_lo, NU)
                if k >= 2:
                    act.wait_ge(g_add, k - 1)
                A((o_sb, o_tmp)[k % 2][:, :], banks[BANK[i]], ACT.Tanh, scale=hrs[:, t:t + 1]).then_inc(g_tanh, 1)

            def f_square(k):
                _, n, t = [x for x in ITEMS if x[0] == "gate"][k]
                act.wait_ge(g_add, k + 1)
                act.wait_ge(f_sq, k) if k else act.wait_ge(h_sq, ST * NH)
                A(sq[:, 1, :], h[:, t, n * SEQ:(n + 1) * SEQ], ACT.Square, accum_out=fsq[:, t, n:n + 1]).then_inc(f_sq, 1)

            act.dma_start(gm[:, :], g_mix).then_inc(gm_in, 16)
            for kt in range(KT):
                act.dma_start(xt_raw[:, kt, :], x_t[kt * P:(kt + 1) * P, :]).then_inc(xt_in[kt], 16)
            act.dma_start(cst[:, :], consts).then_inc(cst_in, 16)
            act.dma_start(rope_r, rope.rearrange("b p c -> p b c")).then_inc(rope_in, 16)
            act.dma_start(lam_in[:, :, :], lams.partition_broadcast(P)).then_inc(small_in, 16)
            act.dma_start(gp[:, :], g_ple).then_inc(small_in, 16)
            act.dma_start(gs[:, :], g_subln).then_inc(small_in, 16)
            act.dma_start(gfin[:, :], g_final.partition_broadcast(P)).then_inc(small_in, 16)

            act.wait_ge(gm_in, 16)
            for kt in range(KT):
                act.wait_ge(xt_in[kt], 16)
                A(usplit[:, 0, kt, :], xt_raw[:, kt, :], ACT.Copy, scale=gm[:, kt:kt + 1]).then_inc(u_hi, 1)
                if kt == 2:
                    weights_hi(0)
                if kt % 2 == 1 and kt > 1:
                    act.wait_ge(u_lo, kt - 2)
                    A(xt_raw[:, kt - 3, :], xt_raw[:, kt - 3, :], ACT.Square).then_inc(x_sq, 1)
            weights_hi(1)
            for kt in (KT - 2,):
                act.wait_ge(u_lo, kt + 1)
                A(xt_raw[:, kt, :], xt_raw[:, kt, :], ACT.Square).then_inc(x_sq, 1)
            weights_hi(2)
            act.wait_ge(x_ms, 1)
            act.wait_ge(set_done, 1)
            A(rstd, ou[:, 1, :], ACT.Sqrt, bias=eps[:, 0:1], scale=1.0 / D_MODEL).then_inc(x_std, 1)
            act.wait_ge(lam_sum, 1)
            A(lam_e[:, :], lam_s[:, :], ACT.Exp).then_inc(lam_exp, 1)

            for u in range(NU):
                if u >= 2:
                    probs_hi(u - 2, 1)
                weights_hi(4 * u + 3)
                if u >= 3:
                    y_round(u - 3)
                if u >= 2:
                    probs_hi(u - 2, 2)
                if u >= 1:
                    exponentials(u - 1, 0)
                weights_hi(4 * u + 4)
                if u >= 1:
                    exponentials(u - 1, 1)
                if u >= 2:
                    output_copy(u - 2)
                z_gate(u)
                weights_hi(4 * u + 5)
                if u >= 1:
                    exponentials(u - 1, 2)
                    probs_hi(u - 1, 0)
                if u - 2 >= MOBA_UNITS:
                    output_std(u - 2)
                if u >= 1:
                    values_hi(u - 1)
                qk_stack_hi(u)
                weights_hi(4 * u + 6)
            embed_read(0), embed_read(1)
            probs_hi(NU - 2, 1)
            y_round(NU - 3)
            embed_read(2)
            weights_hi(T_OUT)
            exponentials(NU - 1, 0)
            embed_read(3)
            probs_hi(NU - 2, 2)
            weights_hi(T_OUT + 1)
            embed_read(4)
            exponentials(NU - 1, 1)
            embed_read(5)
            output_copy(NU - 2)
            exponentials(NU - 1, 2)
            probs_hi(NU - 1, 0)
            embed_read(6), embed_read(7)
            output_std(NU - 2)
            values_hi(NU - 1)
            weights_hi(T_OUT + 2)
            probs_hi(NU - 1, 1)
            weights_hi(T_OUT + 3)
            y_round(NU - 2)
            probs_hi(NU - 1, 2)
            output_copy(NU - 1)
            output_std(NU - 1)
            weights_hi(T_OUT + 4), weights_hi(T_OUT + 5)
            y_round(NU - 1)
            for j in range(T_OUT + 6, T_GATE + KT // 2):
                weights_hi(j)
            for k in range(7):
                h_square(k)
            for k in (0, 1):
                h_turned_hi(k)
            h_square(7)
            for k in (2, 3):
                h_turned_hi(k)
            for j in range(T_GATE + KT // 2, T_ALL):
                weights_hi(j)
            gate_tanh(0)
            h_turned_hi(4), h_turned_hi(5)
            gate_tanh(1)
            h_turned_hi(6), h_turned_hi(7)
            for k in range(2, 2 * ST):
                f_square(k - 2)
                gate_tanh(k)
            f_square(2 * ST - 2)
            f_square(2 * ST - 1)

        @block.vector
        def _(dve):
            V_ = nc.vector

            def weights_lo(j):
                dve.wait_ge(w_hi, j + 1)
                hi, lo = split_target(j)
                if j < T_GATE:
                    V_.tensor_tensor(lo, raw[:, j % RAW, :], hi.bitcast(f32), ALU.subtract).then_inc(w_lo, 1)
                else:
                    for k in range(2):
                        kt, c = 2 * ((j - T_GATE) % (KT // 2)) + k, slice(k * SEQ, (k + 1) * SEQ)
                        last = V_.scalar_tensor_tensor(lo[:, c], raw[:, j % RAW, c], gp[:, kt:kt + 1], hi[:, c].bitcast(f32),
                                                       ALU.mult, ALU.subtract)
                    last.then_inc(w_lo, 1)

            def rope_start(u, t):
                n = 2 * u + t
                dve.wait_ge(proj, 4 * u + t + 1)
                if u:
                    dve.wait_ge(roped, n - 1)
                    dve.wait_ge(qk_lo, u)
                o = pj[:, (4 * u + t) % 2, :]
                V_.stream_shuffle(shuf[:, t, :], o, [*range(8, 16), *range(8), *range(16, 32)])
                V_.tensor_tensor(rot[:, t, :], o, rope_r[:, 0, :], ALU.mult).then_inc(pj_read, 1)

            def z_scale(u):
                dve.wait_ge(proj, 4 * u + Z + 1)
                if u >= 3:
                    dve.wait_ge(y_ready, u - 2)
                V_.scalar_tensor_tensor(zbuf[:, u % 3, :], pj[:, (4 * u + Z) % 2, :], 0.5, rstd, ALU.mult, ALU.mult).then_inc(pj_read, 1)

            def z_silu(u):
                dve.wait_ge(z_tanh, u + 1)
                V_.scalar_tensor_tensor(zbuf[:, u % 3, :], ztanh, 1.0, zbuf[:, u % 3, :], ALU.add, ALU.mult).then_inc(z_done, 1)

            def v_scale(u):
                dve.wait_ge(proj, 4 * u + V + 1)
                if u:
                    dve.wait_ge(vtrans, u)
                V_.tensor_tensor(v_t[:, :], pj[:, (4 * u + V) % 2, :], rstd, ALU.mult).then_inc(pj_read, 1)

            def maxima(u, step):
                n = 3 * u + step
                dve.wait_ge(scores, n + 1)
                d = sc[:, :, 0:SEQ].rearrange("p m (b c) -> p m b c", c=P)
                if step == 0:
                    for m in range(2):
                        last = V_.tensor_tensor(d[:, m, 0:3:2, :], d[:, m, 0:3:2, :], mask.unsqueeze(1).broadcast_to([P, 2, P]), ALU.add)
                    last.then_inc(masked, 1)
                else:
                    b = STEP_W[step] // P - 1
                    V_.tensor_tensor(d[:, :, b, :], d[:, :, b, :], mask.unsqueeze(1).broadcast_to([P, 2, P]), ALU.add).then_inc(masked, 1)
                dve.wait_ge(masked, n + 1)
                c = 0
                for q in STEP_TILES[step]:
                    last = V_.tensor_reduce(nmax[:, q, :], sc[:, :, c:c + (q + 1) * P], AX.X, ALU.max, negate=True)
                    c += (q + 1) * P
                last.then_inc(maxes, 1)

            def reciprocals(u, step):
                n, tiles = 3 * u + step, slice(STEP_TILES[step][0], STEP_TILES[step][-1] + 1)
                dve.wait_ge(exps, n + 1)
                if u:
                    dve.wait_ge(probs_ready, n - 2)
                V_.reciprocal(rinv[:, tiles, :], rsum[:, tiles, :]).then_inc(recips, 1)
                if u >= MOBA_UNITS:
                    k = n - STEPS * MOBA_UNITS
                    if k == 0:
                        dve.wait_ge(lam_done, 1)
                    dve.wait_ge(recips, n + 1 + k)
                    V_.tensor_scalar(rinv[:, tiles, 1:2], rinv[:, tiles, 1:2], nlam[:, 0:1], None, ALU.mult).then_inc(recips, 1)

            def combine(u, step):
                n = 3 * u + step
                dve.wait_ge(weighted, n - STEPS * MOBA_UNITS + 1)
                c = STEP_COL[step]
                for q in STEP_TILES[step]:
                    w = slice(c, c + (q + 1) * P)
                    last = V_.scalar_tensor_tensor(probs[:, 0, w], probs[:, 0, w], rinv[:, q, 0:1], probs[:, 1, w], ALU.mult, ALU.add)
                    c += (q + 1) * P
                last.then_inc(probs_ready, 1)

            def probs_lo(u, step):
                dve.wait_ge(p_hi, 3 * u + step + 1)
                moba = u < MOBA_UNITS
                for (src, dst), (_, hi) in zip(per_map(pt_views(pt_lo, step), moba), per_map(pt_views(pt_hi, step), moba)):
                    last = V_.tensor_tensor(dst, src, hi.bitcast(f32), ALU.subtract)
                last.then_inc(p_lo, 1)

            def qk_stack_lo(u):
                dve.wait_ge(qk_hi, u + 1)
                q, k = rot[:, 0, :], rot[:, 1, :]
                V_.scalar_tensor_tensor(qs[HALF:P, 0, :], q[0:HALF], SCALE, qs[0:HALF, 0, :].bitcast(f32), ALU.mult, ALU.subtract)
                V_.scalar_tensor_tensor(qs[0:HALF, 1, :], q[HALF:P], SCALE, qs[HALF:P, 1, :].bitcast(f32), ALU.mult, ALU.subtract)
                for m in range(2):
                    a = slice(m * HALF, (m + 1) * HALF)
                    for half in range(2):
                        last = V_.tensor_tensor(k_lo[half * HALF:(half + 1) * HALF, m, :], k[a], k_hi[a, m, :].bitcast(f32), ALU.subtract)
                last.then_inc(qk_lo, 1)

            def values_lo(u):
                dve.wait_ge(v_hi, u + 1)
                if u < MOBA_UNITS:
                    v = vsplit[:, :, :].rearrange("p k (m i d) -> p k m i d", m=2, i=2)
                    src = ou[:, 0, :].rearrange("p (k m d) -> p k m d", k=ST, m=2)
                    for m in range(2):
                        last = V_.tensor_tensor(v[:, :, m, 1, :], src[:, :, m, :], v[:, :, m, 0, :].bitcast(f32), ALU.subtract)
                    last.then_inc(v_lo, 1)
                else:
                    src = ou[:, 0, :].rearrange("p (k d) -> p k d", k=ST)
                    V_.tensor_tensor(vsplit[:, :, P:2 * P], src, vsplit[:, :, 0:P].bitcast(f32), ALU.subtract).then_inc(v_lo, 1)

            def output_sum(u):
                dve.wait_ge(o_half, u + 1)
                if u:
                    dve.wait_ge(y_lo, u)
                V_.tensor_tensor(o_sb[0:HALF, :], ou[0:HALF, 0, :], o_tmp[0:HALF, :], ALU.add)
                V_.tensor_tensor(o_sb[HALF:P, :], ou[HALF:P, 1, :], o_tmp[HALF:P, :], ALU.add).then_inc(o_read, 1)

            def output_norm(u):
                k = u - MOBA_UNITS
                dve.wait_ge(o_std, k + 1)
                V_.reciprocal(o_tmp[:, :], o_tmp[:, :]).then_inc(o_inv, 1)
                dve.wait_ge(o_inv, k + 1)
                if k == 0:
                    dve.wait_ge(gs_done, 1)
                V_.scalar_tensor_tensor(o_sb[:, :], o_sb[:, :], gs8[:, 0:1], o_tmp[:, :], ALU.mult, ALU.mult).then_inc(o_read, 1)

            def y_rest(u):
                dve.wait_ge(y_hi, u + 1)
                V_.tensor_tensor(ysplit[:, 1, u, :], o_sb[:, :], ysplit[:, 0, u, :].bitcast(f32), ALU.subtract).then_inc(y_lo, 1)

            def residual(k):
                i = [x for x in range(len(ITEMS)) if ITEMS[x][0] == "out"][k]
                _, n, t = ITEMS[i]
                dve.wait_ge(item, i + 1)
                if n == 0:
                    dve.wait_ge(x_in[t], 16)
                c = slice(n * SEQ, (n + 1) * SEQ)
                V_.tensor_tensor(h[:, t, c], banks[BANK[i]], h[:, t, c], ALU.add).then_inc(h_read, 1)

            def h_turned_lo(k):
                i = [x for x in range(len(ITEMS)) if ITEMS[x][0] == "turn"][k]
                _, n, t = ITEMS[i]
                dve.wait_ge(ht_hi, k + 1)
                a = (slice(None), slice(4 * n, 4 * n + 4), slice(t * P, (t + 1) * P))
                V_.tensor_tensor(usplit[:, 1, a[1], a[2]], banks[BANK[i]].rearrange("p (b c) -> p b c", b=4),
                                 usplit[:, 0, a[1], a[2]].bitcast(f32), ALU.subtract).then_inc(ht_lo, 1)

            def gate_add(k):
                _, n, t = [x for x in ITEMS if x[0] == "gate"][k]
                g, c = (o_sb, o_tmp)[k % 2][:, :], slice(n * SEQ, (n + 1) * SEQ)
                dve.wait_ge(g_tanh, k + 1)
                V_.scalar_tensor_tensor(g, g, 1.0, pe[:, t, c], ALU.add, ALU.mult).then_inc(g_mul, 1)
                dve.wait_ge(g_mul, k + 1)
                V_.tensor_tensor(h[:, t, c], h[:, t, c], g, ALU.add).then_inc(g_add, 1)

            def final_scale(t):
                dve.wait_ge(f_rstd, t + 1)
                V_.scalar_tensor_tensor(h[:, t, :], h[:, t, :], frs[:, t:t + 1], gfin[:, :], ALU.mult, ALU.mult).then_inc(f_out, 1)

            V_.memset(eps[:, :], EPS).then_inc(set_done, 1)
            for kt in range(KT):
                dve.wait_ge(u_hi, kt + 1)
                V_.scalar_tensor_tensor(usplit[:, 1, kt, :], xt_raw[:, kt, :], gm[:, kt:kt + 1], usplit[:, 0, kt, :].bitcast(f32),
                                        ALU.mult, ALU.subtract).then_inc(u_lo, 1)
                if kt == 3:
                    weights_lo(0)
            weights_lo(1)
            for kt in range(1, KT):
                dve.wait_ge(x_sq, kt // 2 + 1)
                dve.wait_ge(pool_own, (kt + 1) // 2)
                if kt > 1:
                    dve.wait_ge(x_sum, kt - 1)
                a = xt_raw[:, 0, :] if kt == 1 else sq[:, 0, :]
                V_.tensor_tensor(sq[:, 0, :], a, xt_raw[:, kt, :], ALU.add).then_inc(x_sum, 1)
            weights_lo(2)
            dve.wait_ge(small_in, 64)
            V_.tensor_tensor(lam_pr[:, :, :], lam_in[:, 0:3:2, :], lam_in[:, 1:4:2, :], ALU.mult).then_inc(lam_prod, 1)
            dve.wait_ge(lam_prod, 1)
            V_.tensor_reduce(lam_s[:, :], lam_pr[:, :, :], AX.X, ALU.add).then_inc(lam_sum, 1)
            V_.tensor_scalar(gs8[:, :], gs[:, :], 1.0 - LAMBDA_INIT, None, ALU.mult).then_inc(gs_done, 1)
            dve.wait_ge(x_std, 1)
            V_.reciprocal(rstd, rstd).then_inc(x_rstd, 1)
            dve.wait_ge(x_rstd, 1)
            dve.wait_ge(rope_in, 16)
            for i in range(2):
                last = V_.tensor_tensor(rope_r[:, i, :], rope_r[:, i, :], rstd, ALU.mult)
            last.then_inc(tab_done, 1)
            dve.wait_ge(tab_done, 1)

            def inverses(u, step):
                reciprocals(u, step)
                if u >= MOBA_UNITS:
                    combine(u, step)

            for u in range(NU):
                rope_start(u, Q)
                if u >= 2:
                    probs_lo(u - 2, 1)
                weights_lo(4 * u + 3)
                if u - 3 >= MOBA_UNITS:
                    output_norm(u - 3)
                rope_start(u, K)
                if u >= 2:
                    probs_lo(u - 2, 2)
                if u >= 1:
                    maxima(u - 1, 0)
                    inverses(u - 1, 0)
                if u >= 3:
                    y_rest(u - 3)
                if u == 0:
                    dve.wait_ge(lam_exp, 1)
                    V_.tensor_scalar(nlam[:, :], lam_e[:, 1:2], lam_e[:, 0:1], LAMBDA_INIT, ALU.subtract, ALU.subtract).then_inc(lam_done, 1)
                weights_lo(4 * u + 4)
                z_scale(u)
                if u >= 1:
                    maxima(u - 1, 1)
                    inverses(u - 1, 1)
                if 0 <= u - 2 < MOBA_UNITS:
                    output_sum(u - 2)
                z_silu(u)
                weights_lo(4 * u + 5)
                if u >= 1:
                    maxima(u - 1, 2)
                    probs_lo(u - 1, 0)
                    values_lo(u - 1)
                v_scale(u)
                if u >= 1:
                    inverses(u - 1, 2)
                qk_stack_lo(u)
                weights_lo(4 * u + 6)
            probs_lo(NU - 2, 1)
            output_norm(NU - 3)
            y_rest(NU - 3)
            weights_lo(T_OUT)
            maxima(NU - 1, 0)
            inverses(NU - 1, 0)
            probs_lo(NU - 2, 2)
            weights_lo(T_OUT + 1)
            maxima(NU - 1, 1)
            inverses(NU - 1, 1)
            maxima(NU - 1, 2)
            probs_lo(NU - 1, 0)
            inverses(NU - 1, 2)
            values_lo(NU - 1)
            weights_lo(T_OUT + 2)
            probs_lo(NU - 1, 1)
            weights_lo(T_OUT + 3)
            output_norm(NU - 2)
            probs_lo(NU - 1, 2)
            y_rest(NU - 2)
            output_norm(NU - 1)
            weights_lo(T_OUT + 4), weights_lo(T_OUT + 5)
            y_rest(NU - 1)
            for j in range(T_OUT + 6, T_GATE):
                weights_lo(j)
            for k in range(4):
                residual(k)
            for j in range(T_GATE, T_GATE + KT // 2):
                weights_lo(j)
            for k in range(4, 7):
                residual(k)
            h_turned_lo(0), h_turned_lo(1)
            residual(7)
            h_turned_lo(2), h_turned_lo(3)
            for j in range(T_GATE + KT // 2, T_ALL):
                weights_lo(j)
            h_turned_lo(4), h_turned_lo(5)
            gate_add(0)
            h_turned_lo(6), h_turned_lo(7)
            for k in range(1, 2 * ST):
                gate_add(k)
                if k > ST:
                    final_scale(k - ST - 1)
            final_scale(ST - 1)

        @block.gpsimd
        def _(pool):
            G = nc.gpsimd
            own = [0]

            def link(ins):
                own[0] += 1
                ins.then_inc(pool_own, 1)
                pool.wait_ge(pool_own, own[0])

            def rope_finish(u, t):
                pool.wait_ge(pj_read, 4 * u + t + 1)
                pool.wait_ge(tab_done, 1)
                link(G.tensor_tensor(shuf[:, t, :], shuf[:, t, :], rope_r[:, 1, :], ALU.mult))
                G.tensor_tensor(rot[:, t, :], rot[:, t, :], shuf[:, t, :], ALU.add).then_inc(roped, 1)

            def normalise(u, step):
                n = 3 * u + step
                moba = u < MOBA_UNITS
                pool.wait_ge(recips, n + 1 if moba else 2 * n + 2 - STEPS * MOBA_UNITS)
                c = STEP_COL[step]
                for q in STEP_TILES[step]:
                    w = slice(c, c + (q + 1) * P)
                    for m in (0, 1) if moba else (1,):
                        last = G.tensor_scalar(probs[:, m, w], probs[:, m, w], rinv[:, q, m:m + 1], 1.0, ALU.mult, ALU.mult)
                    c += (q + 1) * P
                last.then_inc(probs_ready if moba else weighted, 1)

            def output_square(u):
                pool.wait_ge(o_half, u + 1)
                G.tensor_tensor(o_tmp[:, :], o_sb[:, :], o_sb[:, :], ALU.mult).then_inc(o_sq, 1)

            def gate_output(u):
                pool.wait_ge(o_read, u + 1)
                pool.wait_ge(z_done, u + 1)
                G.tensor_tensor(o_sb[:, :], o_sb[:, :], zbuf[:, u % 3, :], ALU.mult).then_inc(y_ready, 1)

            def inverse_rms(to, a, b, tmp, done, half):
                link(G.tensor_tensor(tmp, a, b, ALU.add))
                link(G.tensor_scalar(tmp, tmp, 1.0 / D_MODEL, EPS, ALU.mult, ALU.add))
                if half:
                    link(G.tensor_tensor(tmp, tmp, mhalf[:, 0:tmp.shape[1]], ALU.pow))
                    G.tensor_scalar(to, tmp, 0.5, 1.0, ALU.mult, ALU.mult).then_inc(done, 1)
                else:
                    G.tensor_tensor(to, tmp, mhalf[:, 0:tmp.shape[1]], ALU.pow).then_inc(done, 1)

            for kt in range(1, KT, 2):
                pool.wait_ge(u_lo, kt + 1)
                own[0] += 1
                G.tensor_tensor(xt_raw[:, kt, :], xt_raw[:, kt, :], xt_raw[:, kt, :], ALU.mult).then_inc(pool_own, 1)
            link(G.memset(mhalf[:, :], -0.5))

            for u in range(NU + 2):
                if u < NU:
                    rope_finish(u, Q)
                if u >= 3:
                    gate_output(u - 3)
                if 1 <= u <= NU:
                    normalise(u - 1, 0)
                if u < NU:
                    rope_finish(u, K)
                if 1 <= u <= NU:
                    normalise(u - 1, 1)
                if u - 2 >= MOBA_UNITS:
                    output_square(u - 2)
                if 1 <= u <= NU:
                    normalise(u - 1, 2)
            gate_output(NU - 1)
            pool.wait_ge(h_sq, ST * NH)
            inverse_rms(hrs[:, :], ssq[:, :, 0], ssq[:, :, 1], ssa[:, :], h_rstd, True)
            for t in range(ST):
                pool.wait_ge(f_sq, ST + t + 1)
                inverse_rms(frs[:, t:t + 1], fsq[:, t, 0:1], fsq[:, t, 1:2], fsa[:, t:t + 1], f_rstd, False)


def kernel(**inputs):
    import concourse.bacc as bacc
    from concourse.bass_utils import run_bass_kernel_spmd as run

    a = {k: np.asarray(v) for k, v in inputs.items()}
    units = D_MODEL // P
    starts = []
    for u in range(units):
        part, q = (0, u) if u < units // 2 else (3, u - units // 2)
        starts += [(part + i) * 512 + q * P for i in (0, 1)] + [3072 + u * P, (part + 2) * 512 + q * P]
    w = a["w_in"][0].reshape(D_MODEL // P, P, -1)
    w_in = np.stack([w[:, :, c:c + P] for c in starts])
    w_in = w_in.reshape(units, 4, D_MODEL // P, P, P).transpose(0, 3, 1, 2, 4)

    inv = np.float32(ROPE_THETA) ** (-np.arange(0, ROPE_DIM, 2, dtype=np.float32) / np.float32(ROPE_DIM))
    ang = inv[:, None] * np.arange(SEQ, dtype=np.float32)[None, :]
    rope = np.zeros((2, P, SEQ), np.float32)
    rope[0] = 1.0
    for b in range(0, P, HEAD_DIM):
        rope[0, b:b + ROPE_DIM] = np.tile(np.cos(ang), (2, 1))
        rope[1, b:b + ROPE_DIM] = np.concatenate([-np.sin(ang), np.sin(ang)])
    consts = np.concatenate([np.eye(P), np.where(np.tri(P) > 0, 0.0, -3e38), np.ones((P, P))], 1).astype(np.float32)

    arrays = {
        "x_t": a["x"][0].T, "x": a["x"][0], "p_t": a["p"][0, 0].T,
        "w_in": w_in.reshape(units, P, 4, D_MODEL), "w_out": a["w_out"][0], "w_gate": a["w_ple_gate"][0], "w_ple": a["w_ple"][0],
        "g_mix": a["g_mix"][0].reshape(-1, P).T, "g_ple": a["g_ple"][0].reshape(-1, P).T,
        "g_subln": a["g_subln"][0].reshape(P, 1), "g_final": a["g_final"],
        "lams": np.stack([a[n][0] for n in ("diff_lq1", "diff_lk1", "diff_lq2", "diff_lk2")]),
        "rope": rope, "consts": consts,
    }
    arrays = {f"in_{k}": np.ascontiguousarray(v) for k, v in arrays.items()}
    nc = bacc.Bacc("TRN2", target_bir_lowering=False, num_devices=1)
    args = [nc.dram_tensor(k, v.shape, mybir.dt.from_np(v.dtype), kind="ExternalInput").ap() for k, v in arrays.items()]
    out = nc.dram_tensor("out", (SEQ, D_MODEL), mybir.dt.float32, kind="ExternalOutput").ap()
    build_program(nc, *args, out)
    r = run(nc, [arrays], core_ids=[0])
    return r.results[0]["out"].reshape(1, SEQ, D_MODEL)
```

```python
import numpy as np
import concourse.bass as bass
from concourse import mybir
from concourse.alu_op_type import AluOpType as ALU
from contextlib import ExitStack

D_MODEL, SEQ, PLE_DIM, HEAD_DIM = 1024, 512, 256, 64
MOBA_HEADS, MOBA_BLOCK, MOBA_TOPK, DIFF_HEADS = 8, 256, 3, 4
ROPE_THETA, ROPE_DIM = 500000.0, 16
EPS = 1e-6
LAMBDA_INIT = 0.8 - 0.6 * 1.0
P = 128
assert min(MOBA_TOPK, SEQ // MOBA_BLOCK) == SEQ // MOBA_BLOCK


def build_program(nc, x_t, x, p_t, w_in, w_out, w_gate, w_ple, g_mix, g_ple, g_subln, g_final, lams,
                  rope, consts, out):
    f32, f32r = mybir.dt.float32, mybir.dt.float32r
    ACT = mybir.ActivationFunctionType
    AX = mybir.AxisListType

    KT = D_MODEL // P
    ST = SEQ // P
    NU = D_MODEL // P
    MOBA_UNITS = MOBA_HEADS * HEAD_DIM // P
    NH = D_MODEL // SEQ
    HALF = HEAD_DIM
    Q, K, Z, V = range(4)
    STEPS = 3
    STEP_TILES = [(0, 1), (2,), (3,)]
    STEP_COL = [0, 384, 768]
    STEP_W = [384, 384, 512]
    PT_BLOCKS = 12
    SCALE = float(HEAD_DIM) ** -0.5

    T_IN = 0
    T_PLE = T_IN + 4 * NU
    T_P = T_PLE + 2
    T_OUT = T_P + 1
    T_GATE = T_OUT + NH * KT // 2
    T_ALL = T_GATE + NH * KT // 2
    RAW = 4

    ctx = ExitStack()
    with ctx:
        def sb(name, shape, dt=f32):
            return ctx.enter_context(nc.sbuf_tensor(name, shape, dt))

        def sem(name):
            return ctx.enter_context(nc.semaphore(name))

        wsplit = sb("wsplit", [P, 4, 2, 1024], f32r)
        usplit = sb("usplit", [P, 2, KT, SEQ], f32r)
        csplit = sb("csplit", [P, 9216], f32r)
        ysplit = sb("ysplit", [P, 2, NU, SEQ], f32r)
        qksplit = sb("qksplit", [P, 2, 2, SEQ], f32r)
        vsplit = sb("vsplit", [P, ST, 2 * P], f32r)
        pt_hi = csplit[:, 0:3072].rearrange("p (m c) -> p m c", m=2)
        pt_lo = csplit[:, 3072:6144].rearrange("p (m c) -> p m c", m=2)
        qs = csplit[:, 6144:7168].rearrange("p (m c) -> p m c", m=2)
        kst = csplit[:, 7168:9216].rearrange("p (i m c) -> p i m c", i=2, m=2)
        k_hi = csplit[:, 7168:8192].rearrange("p (m c) -> p m c", m=2)
        k_lo = csplit[:, 8192:9216].rearrange("p (m c) -> p m c", m=2)
        wout_n = [usplit[:, :, :, :].rearrange("p s k c -> p (s k c)"),
                  wsplit[:, :, :, :].rearrange("p a s c -> p (a s c)")]
        wgate_n = [csplit[:, 0:8192], wsplit[:, :, :, :].rearrange("p a s c -> p (a s c)")]

        def chunk(region, c):
            v = region.rearrange("p (c s n) -> p c s n", c=KT // 2, s=2)
            return v[:, c, 0, :], v[:, c, 1, :]

        def chunk_tile(region, kt):
            hi, lo = chunk(region, kt // 2)
            o = (kt % 2) * SEQ
            return hi[:, o:o + SEQ], lo[:, o:o + SEQ]

        raw = sb("raw", [P, RAW, 1024])
        hbuf = sb("hbuf", [P, 4096])
        tbuf = sb("tbuf", [P, 4096])
        xt_raw = hbuf[:, :].rearrange("p (k c) -> p k c", k=KT)
        probs = hbuf[:, 0:2560].rearrange("p (m c) -> p m c", m=2)
        zbuf = hbuf[:, 2560:4096].rearrange("p (b c) -> p b c", b=3)
        h = hbuf[:, :].rearrange("p (s d) -> p s d", s=ST)
        shuf = tbuf[:, 0:1024].rearrange("p (b c) -> p b c", b=2)
        rot = tbuf[:, 1024:2048].rearrange("p (b c) -> p b c", b=2)
        rope_r = tbuf[:, 2048:3072].rearrange("p (b c) -> p b c", b=2)
        rstd = tbuf[:, 3072:3584]
        ztanh = tbuf[:, 3584:4096]
        pe = tbuf[:, :].rearrange("p (s d) -> p s d", s=ST)
        v_t = sb("v_t", [P, SEQ])
        o_sb = sb("o_sb", [P, SEQ])
        o_tmp = sb("o_tmp", [P, SEQ])
        xsum = sb("xsum", [P, SEQ])
        gfin = sb("gfin", [P, D_MODEL])
        cst = sb("cst", [P, 3 * P])
        ident, mask, ones = cst[:, 0:P], cst[:, P:2 * P], cst[:, 2 * P:3 * P]
        gm = sb("gm", [P, KT])
        gp = sb("gp", [P, KT])
        gs = sb("gs", [P, 1])
        gs8 = sb("gs8", [P, 1])
        lam_in = sb("lam_in", [P, 4, HEAD_DIM])
        lam_pr = sb("lam_pr", [P, 2, HEAD_DIM])
        lam_s = sb("lam_s", [P, 2])
        lam_e = sb("lam_e", [P, 2])
        nlam = sb("nlam", [P, 1])
        rms4 = sb("rms4", [P, ST])
        mhalf = sb("mhalf", [P, ST])
        nmax = sb("nmax", [P, ST, 2])
        rsum = sb("rsum", [P, ST, 2])
        rinv = sb("rinv", [P, ST, 2])
        ssq = sb("ssq", [P, ST, 2])
        ssa = sb("ssa", [P, ST])
        hrs = sb("hrs", [P, ST])
        fsq = sb("fsq", [P, ST, 2])
        fsa = sb("fsa", [P, ST])
        frs = sb("frs", [P, ST])

        def ps(name):
            return ctx.enter_context(nc.psum_tensor(name, [P, 2, SEQ], f32))

        pj, sc, tr, ou = ps("pj"), ps("sc"), ps("tr"), ps("ou")
        banks = [pj[:, 0, :], pj[:, 1, :], sc[:, 0, :], sc[:, 1, :],
                 tr[:, 0, :], tr[:, 1, :], ou[:, 0, :], ou[:, 1, :]]

        raw_in = [sem(f"raw_in{i}") for i in range(RAW)]
        w0_in = [sem(f"w0_in{i}") for i in range(4)]
        xt_in = [sem(f"xt_in{k}") for k in range(KT)]
        x_in = [sem(f"x_in{t}") for t in range(ST)]
        gm_in, w0_hi, w0_lo, small_in, cst_in, rope_in, stored = [sem(n) for n in "gm_in w0_hi w0_lo small_in cst_in rope_in stored".split()]
        u_hi, u_lo, x_sq, x_sum, x_ms, x_mean, x_rstd, x_wide, x_bc, rstd_done, tab_done = [
            sem(n) for n in "u_hi u_lo x_sq x_sum x_ms x_mean x_rstd x_wide x_bc rstd_done tab_done".split()]
        lam_prod, lam_sum, lam_exp, lam_done, gs_done = [
            sem(n) for n in "lam_prod lam_sum lam_exp lam_done gs_done".split()]
        w_hi, w_lo, proj, pj_read, turned, roped, qk_hi, qk_lo, stacked = [
            sem(n) for n in "w_hi w_lo proj pj_read turned roped qk_hi qk_lo stacked".split()]
        scores, masked, maxes, exps, recips, weighted, probs_ready, ptrans, p_hi, p_lo = [
            sem(n) for n in "scores masked maxes exps recips weighted probs_ready ptrans p_hi p_lo".split()]
        vtrans, v_hi, v_lo, pv, o_half, o_read, o_sq, o_ms, o_mean, o_rstd, o_wide, o_bc = [
            sem(n) for n in "vtrans v_hi v_lo pv o_half o_read o_sq o_ms o_mean o_rstd o_wide o_bc".split()]
        z_tanh, z_done, y_ready, y_hi, y_lo = [sem(n) for n in "z_tanh z_done y_ready y_hi y_lo".split()]
        pe_mm, pe_read, item, h_read, h_sq, h_rstd, ht_hi, ht_lo = [
            sem(n) for n in "pe_mm pe_read item h_read h_sq h_rstd ht_hi ht_lo".split()]
        g_tanh, g_mul, g_add, f_sq, f_rstd, f_out, pool_own = [
            sem(n) for n in "g_tanh g_mul g_add f_sq f_rstd f_out pool_own".split()]

        def pj_bank(j):
            return sc[:, j - 2, :] if j in (Z, V) else pj[:, j % 2, :]

        def split_target(j):
            if j < T_OUT:
                return wsplit[:, j % 4, 0, :], wsplit[:, j % 4, 1, :]
            t, region = (j - T_OUT, wout_n) if j < T_GATE else (j - T_GATE, wgate_n)
            return chunk(region[t // (KT // 2)], t % (KT // 2))

        def pt_blocks(step):
            return [[(0, 0, 1, 2), (2, 5, 1, 1)], [(0, 2, 4, 3)], [(0, 3, 4, 3), (3, 8, 1, 1)]][step]

        def pt_views(store, step):
            for first, to, stride, n in pt_blocks(step):
                src = tr[:, :, first * P:(first + n) * P].rearrange("p m (b c) -> p m b c", b=n)
                dst = store.rearrange("p m (b c) -> p m b c", c=P)[:, :, to:to + stride * (n - 1) + 1:stride, :]
                yield src, dst

        def per_map(pairs, moba):
            for src, dst in pairs:
                for m in range(2 if moba else 1):
                    yield src[:, m], dst[:, m]

        ITEMS = ([("out", 0, t) for t in range(ST)] + [("out", 1, 0), ("out", 1, 1), ("out", 1, 2), ("turn", 0, 0), ("turn", 1, 0),
                 ("out", 1, 3), ("turn", 0, 1), ("turn", 1, 1), ("gate", 0, 0), ("turn", 0, 2), ("turn", 1, 2), ("gate", 0, 1),
                 ("turn", 0, 3), ("turn", 1, 3), ("gate", 0, 2), ("gate", 0, 3)] + [("gate", 1, t) for t in range(ST)])
        BANK = list(range(7)) + [(0, 1, 7, 2, 3, 4, 5, 6)[i % 8] for i in range(len(ITEMS) - 7)]

        def nth(i):
            return sum(k[0] == ITEMS[i][0] for k in ITEMS[:i + 1])

        def number(kind, n, t):
            return ITEMS.index((kind, n, t))

        block = ctx.enter_context(nc.Block())

        @block.sync
        def _(sp):
            def load_tile(j):
                if j == RAW:
                    sp.wait_ge(w0_lo, 4)
                elif j > RAW:
                    sp.wait_ge(w_lo, j - RAW)
                dst, halves = raw[:, j % RAW, :], raw[:, j % RAW, :].rearrange("p (k c) -> p k c", k=2)
                if j == 0:
                    for c in range(4):
                        w = slice(256 * c, 256 * c + 256)
                        sp.dma_start(dst[:, w], w_in[0, :, 0, w]).then_inc(w0_in[c], 16)
                        for k in (1,) if c == 0 else (3,) if c == 1 else (2 * c, 2 * c + 1):
                            sp.dma_start(xt_raw[:, k, :], x_t[k * P:(k + 1) * P, :]).then_inc(xt_in[k], 16)
                    return
                if j < T_PLE:
                    src = w_in[j // 4, :, j % 4, :]
                elif j < T_P:
                    src = w_ple[(j - T_PLE) * P:(j - T_PLE + 1) * P, :]
                elif j < T_OUT:
                    dst, src = halves, p_t.rearrange("(k p) c -> p k c", k=2)
                else:
                    w, t = (w_out, j - T_OUT) if j < T_GATE else (w_gate, j - T_GATE)
                    n, c = divmod(t, KT // 2)
                    dst = halves
                    src = w[2 * c * P:(2 * c + 2) * P, n * SEQ:(n + 1) * SEQ].rearrange("(k p) c -> p k c", k=2)
                sp.dma_start(dst, src).then_inc(raw_in[j % RAW], 16)

            def stack_qk(u):
                sp.wait_ge(qk_lo, 2 * u + 2)
                if u:
                    sp.wait_ge(scores, 3 * u)
                for m in range(2):
                    a = slice(m * HALF, (m + 1) * HALF)
                    for i in range(2):
                        to = slice(i * HALF, (i + 1) * HALF)
                        sp.dma_start(qs[to, m, :].bitcast(f32), qksplit[a, 0, i, :].bitcast(f32)).then_inc(stacked, 16)
                        sp.dma_start(kst[to, :, m, :].bitcast(f32), qksplit[a, 1, :, :].bitcast(f32)).then_inc(stacked, 16)

            for j in range(T_GATE):
                load_tile(j)
                if j == 1:
                    sp.dma_start(cst[:, :], consts).then_inc(cst_in, 16)
                elif j == 3:
                    sp.dma_start(rope_r, rope.rearrange("b p c -> p b c")).then_inc(rope_in, 16)
                    sp.dma_start(lam_in[:, :, :], lams.partition_broadcast(P)).then_inc(small_in, 16)
                    sp.dma_start(gp[:, :], g_ple).then_inc(small_in, 16)
                    sp.dma_start(gs[:, :], g_subln).then_inc(small_in, 16)
                    sp.dma_start(gfin[:, :], g_final.partition_broadcast(P)).then_inc(small_in, 16)
                if j % 4 == 1 and 2 <= j // 4 <= NU + 1:
                    stack_qk(j // 4 - 2)
            sp.wait_ge(y_ready, NU)
            for t in range(ST):
                sp.dma_start(h[:, t, :], x[t * P:(t + 1) * P, :]).then_inc(x_in[t], 16)
            for j in range(T_GATE, T_ALL):
                load_tile(j)
            for t in range(ST):
                sp.wait_ge(f_out, t + 1)
                sp.dma_start(out[t * P:(t + 1) * P, :], h[:, t, :]).then_inc(stored, 16)
            sp.wait_ge(stored, 16 * ST)

        @block.tensor
        def _(pe_eng):
            mm = nc.tensor.matmul

            def project(u, t, kts):
                j = 4 * u + t
                if j and kts[0] == 0:
                    pe_eng.wait_ge(w_lo, j)
                if j >= 4 and kts[0] == 0:
                    pe_eng.wait_ge(pj_read, max(j - 1, 4) if j > 5 else j - 3)
                o = pj_bank(j)
                for kt in kts:
                    if j == 0:
                        pe_eng.wait_ge(w0_lo, kt // 2 + 1)
                        pe_eng.wait_ge(u_lo, kt + 1)
                    w_h, w_l = (wsplit[:, j % 4, i, kt * P:(kt + 1) * P] for i in range(2))
                    mm(o, w_h, usplit[:, 0, kt, :], start=kt == 0, stop=False)
                    mm(o, w_h, usplit[:, 1, kt, :], start=False, stop=False)
                    last = mm(o, w_l, usplit[:, 0, kt, :], start=False, stop=kt == KT - 1)
                if kts[-1] == KT - 1:
                    last.then_inc(proj, 1)

            def score(u, step):
                if step == 0:
                    pe_eng.wait_ge(stacked, 128 * (u + 1))
                    if u == 0:
                        pe_eng.wait_ge(pj_read, 4)
                if 3 * u + step:
                    pe_eng.wait_ge(exps, 3 * u + step)
                for m in range(2):
                    c = 0
                    for q in STEP_TILES[step]:
                        n = (q + 1) * P
                        o, w = sc[:, m, c:c + n], qs[:, m, q * P:(q + 1) * P]
                        mm(o, w, k_hi[:, m, 0:n], start=True, stop=False)
                        last = mm(o, w, k_lo[:, m, 0:n], start=False, stop=True)
                        c += n
                last.then_inc(scores, 1)

            def turn_probs(u, step):
                n = 3 * u + step
                pe_eng.wait_ge(probs_ready, n + 1)
                if n:
                    pe_eng.wait_ge(p_lo, n)
                for m in range(2 if u < MOBA_UNITS else 1):
                    for b in range(STEP_W[step] // P):
                        c = STEP_COL[step] + b * P
                        last = nc.tensor.transpose(tr[:, m, b * P:(b + 1) * P], probs[:, m, c:c + P], ident)
                last.then_inc(ptrans, 1)

            def turn_values(u):
                pe_eng.wait_ge(pj_read, 4 * u + V + 1)
                if u:
                    if u - 1 < MOBA_UNITS:
                        pe_eng.wait_ge(o_read, u)
                    else:
                        pe_eng.wait_ge(o_half, u)
                for kt in range(ST):
                    last = nc.tensor.transpose(ou[:, 0, kt * P:(kt + 1) * P], v_t[:, kt * P:(kt + 1) * P], ident)
                last.then_inc(vtrans, 1)

            def weigh_values(u):
                pe_eng.wait_ge(v_lo, u + 1)
                pe_eng.wait_ge(p_lo, 3 * u + 3)
                if u:
                    pe_eng.wait_ge(o_read, u)
                moba = u < MOBA_UNITS
                for m in range(2 if moba else 1):
                    for kt in range(ST):
                        b, n = (5 * kt if kt < 3 else 8) * P, (ST - kt) * P
                        o = ou[:, m, kt * P:SEQ]
                        ph, pl = pt_hi[:, m, b:b + n], pt_lo[:, m, b:b + n]
                        first, end = kt == 0, kt == ST - 1
                        if moba:
                            v = vsplit[:, kt, m * P:(m + 1) * P]
                            mm(o, v, ph, start=first, stop=False)
                            last = mm(o, v, pl, start=False, stop=end)
                        else:
                            mm(o, vsplit[:, kt, 0:P], ph, start=first, stop=False)
                            mm(o, vsplit[:, kt, 0:P], pl, start=False, stop=False)
                            last = mm(o, vsplit[:, kt, P:2 * P], ph, start=False, stop=end)
                last.then_inc(pv, 1)

            def sums_by_token(src, done):
                for t in range(ST):
                    last = mm(ou[:, 1, t:t + 1], src[:, t * P:(t + 1) * P], ones[:, 0:1], start=t == 0, stop=t == ST - 1,
                              skip_group_check=True)
                last.then_inc(done, 1)

            def to_all_partitions(src, done):
                for t in range(ST):
                    last = mm(ou[:, 1, t * P:(t + 1) * P], src[:, t * P:(t + 1) * P], ident, start=True, stop=True)
                last.then_inc(done, 1)

            def square_sum(u):
                pe_eng.wait_ge(o_sq, u - MOBA_UNITS + 1)
                sums_by_token(o_tmp, o_ms)

            def spread_rms(u):
                pe_eng.wait_ge(o_wide, u - MOBA_UNITS + 1)
                to_all_partitions(o_tmp, o_bc)

            def embed(g):
                t, n = divmod(g, NH)
                if g == 0:
                    pe_eng.wait_ge(w_lo, T_OUT - 1)
                if g < 2:
                    pe_eng.wait_ge(pj_read, 4 * NU - 1 + g)
                else:
                    pe_eng.wait_ge(pe_read, g - 1)
                o = pj[:, g % 2, :]
                for kt in range(2):
                    p_h, p_l = (wsplit[:, 2, i, kt * SEQ + t * P:kt * SEQ + (t + 1) * P] for i in range(2))
                    w_h, w_l = (wsplit[:, kt, i, n * SEQ:(n + 1) * SEQ] for i in range(2))
                    mm(o, p_h, w_h, start=kt == 0, stop=False)
                    mm(o, p_h, w_l, start=False, stop=False)
                    last = mm(o, p_l, w_h, start=False, stop=kt == 1)
                last.then_inc(pe_mm, 1)

            def bank_free(i):
                before = [k for k in range(i) if BANK[k] == BANK[i]]
                if before:
                    b = before[-1]
                    pe_eng.wait_ge({"out": h_read, "turn": ht_lo, "gate": g_tanh}[ITEMS[b][0]], nth(b))
                elif BANK[i] < 2:
                    pe_eng.wait_ge(pe_read, ST * NH - 1 + BANK[i])
                elif BANK[i] < 4:
                    pe_eng.wait_ge(exps, STEPS * NU)
                elif BANK[i] < 6:
                    pe_eng.wait_ge(p_lo, STEPS * NU)
                else:
                    pe_eng.wait_ge(o_read, NU)

            def accumulate(i, left, region, kts):
                t = ITEMS[i][2]
                for kt in kts:
                    a_h, a_l = (left[:, k, kt, t * P:(t + 1) * P] for k in range(2))
                    w_h, w_l = chunk_tile(region, kt)
                    mm(banks[BANK[i]], a_h, w_h, start=kt == 0, stop=False)
                    mm(banks[BANK[i]], a_h, w_l, start=False, stop=False)
                    last = mm(banks[BANK[i]], a_l, w_h, start=False, stop=kt == KT - 1)
                if kts[-1] == KT - 1:
                    last.then_inc(item, 1)

            def mix_out(i, kts):
                n = ITEMS[i][1]
                if kts[0] == 0:
                    bank_free(i)
                pe_eng.wait_ge(w_lo, T_OUT + n * KT // 2 + kts[-1] // 2)
                pe_eng.wait_ge(y_lo, kts[-1] + 1)
                accumulate(i, ysplit, wout_n[n], kts)

            def turn_h(i):
                _, n, t = ITEMS[i]
                bank_free(i)
                pe_eng.wait_ge(h_read, nth(number("out", n, t)))
                for b in range(4):
                    c = n * SEQ + b * P
                    last = nc.tensor.transpose(banks[BANK[i]][:, b * P:(b + 1) * P], h[:, t, c:c + P], ident)
                last.then_inc(item, 1)

            def gate(i):
                _, n, t = ITEMS[i]
                bank_free(i)
                pe_eng.wait_ge(w_lo, T_GATE + (n + 1) * KT // 2 - 1)
                pe_eng.wait_ge(ht_lo, nth(number("turn", 1, t)))
                accumulate(i, usplit, wgate_n[n], range(KT))

            lower, upper = range(KT // 2), range(KT // 2, KT)
            for u in range(NU):
                project(u, Q, lower)
                project(u, Q, upper)
                if u >= 2:
                    turn_probs(u - 2, 1)
                project(u, K, lower)
                if u - 3 >= MOBA_UNITS:
                    spread_rms(u - 3)
                project(u, K, upper)
                if u == 0:
                    pe_eng.wait_ge(cst_in, 16)
                    pe_eng.wait_ge(x_sum, KT - 1)
                    sums_by_token(xsum, x_ms)
                if u >= 2:
                    turn_probs(u - 2, 2)
                if u >= 1:
                    score(u - 1, 0)
                project(u, Z, lower)
                project(u, Z, upper)
                if u == 0:
                    pe_eng.wait_ge(x_wide, 1)
                    to_all_partitions(xsum, x_bc)
                if u >= 1:
                    score(u - 1, 1)
                if u >= 2:
                    weigh_values(u - 2)
                project(u, V, lower)
                project(u, V, upper)
                if u >= 1:
                    score(u - 1, 2)
                if u >= 1:
                    turn_probs(u - 1, 0)
                if u - 2 >= MOBA_UNITS:
                    square_sum(u - 2)
                if u >= 1:
                    turn_values(u - 1)
            embed(0)
            embed(1)
            turn_probs(NU - 2, 1)
            spread_rms(NU - 3)
            embed(2)
            score(NU - 1, 0)
            embed(3)
            turn_probs(NU - 2, 2)
            embed(4)
            score(NU - 1, 1)
            embed(5)
            weigh_values(NU - 2)
            score(NU - 1, 2)
            turn_probs(NU - 1, 0)
            embed(6)
            embed(7)
            square_sum(NU - 2)
            turn_values(NU - 1)
            mix_out(0, range(0, 2))
            turn_probs(NU - 1, 1)
            mix_out(0, range(2, 4))
            mix_out(0, range(4, 6))
            turn_probs(NU - 1, 2)
            spread_rms(NU - 2)
            mix_out(1, range(0, 2))
            mix_out(1, range(2, 4))
            mix_out(1, range(4, 6))
            weigh_values(NU - 1)
            mix_out(2, range(0, 3))
            mix_out(2, range(3, 6))
            square_sum(NU - 1)
            mix_out(3, range(0, 3))
            mix_out(3, range(3, 6))
            spread_rms(NU - 1)
            for i in range(4):
                mix_out(i, range(6, 7))
            for i in range(4):
                mix_out(i, range(7, 8))
            for i in range(4, len(ITEMS)):
                if ITEMS[i][0] == "out":
                    mix_out(i, range(KT))
                elif ITEMS[i][0] == "turn":
                    turn_h(i)
                else:
                    gate(i)

        @block.scalar
        def _(act):
            A = nc.scalar.activation

            def weights_hi(j):
                act.wait_ge(raw_in[j % RAW], 16 * (j // RAW + (j % RAW > 0)))
                if 4 <= j < T_OUT:
                    act.wait_ge(proj, j - 3)
                elif j >= T_GATE + KT // 2:
                    act.wait_ge(item, 1 + number("out", 1, 3))
                elif j >= T_GATE:
                    act.wait_ge(pv, NU)
                elif j >= T_OUT + KT // 2:
                    act.wait_ge(pe_mm, ST * NH)
                elif j >= T_OUT:
                    act.wait_ge(proj, 4 * NU)
                hi = split_target(j)[0]
                if j < T_GATE:
                    A(hi, raw[:, j % RAW, :], ACT.Copy).then_inc(w_hi, 1)
                else:
                    for k in range(2):
                        kt = 2 * ((j - T_GATE) % (KT // 2)) + k
                        last = A(hi[:, k * SEQ:(k + 1) * SEQ], raw[:, j % RAW, k * SEQ:(k + 1) * SEQ], ACT.Copy, scale=gp[:, kt:kt + 1])
                    last.then_inc(w_hi, 1)

            def exponentials(u, step):
                act.wait_ge(maxes, 3 * u + step + 1)
                if u:
                    act.wait_ge(ptrans, 3 * u + step - 2)
                c = 0
                for q in STEP_TILES[step]:
                    n = (q + 1) * P
                    for m in range(2):
                        last = A(probs[:, m, STEP_COL[step] + c:STEP_COL[step] + c + n], sc[:, m, c:c + n], ACT.Exp,
                                 bias=nmax[:, q, m:m + 1], accum_out=rsum[:, q, m:m + 1])
                    c += n
                last.then_inc(exps, 1)

            def probs_hi(u, step):
                act.wait_ge(ptrans, 3 * u + step + 1)
                if step == 0 and u:
                    act.wait_ge(pv, u)
                for src, dst in per_map(pt_views(pt_hi, step), u < MOBA_UNITS):
                    last = A(dst, src, ACT.Copy)
                last.then_inc(p_hi, 1)

            def qk_hi_of(u, t):
                act.wait_ge(roped, 2 * u + t + 1)
                if u:
                    act.wait_ge(stacked, 128 * u)
                A(qksplit[:, t, 0, :], rot[:, t, :], ACT.Copy, scale=(SCALE, 1.0)[t]).then_inc(qk_hi, 1)

            def values_hi(u):
                act.wait_ge(vtrans, u + 1)
                if u:
                    act.wait_ge(pv, u)
                if u < MOBA_UNITS:
                    dst = vsplit[:, :, :].rearrange("p k (m i d) -> p k m i d", m=2, i=2)[:, :, :, 0, :]
                    src = ou[:, 0, :].rearrange("p (k m d) -> p k m d", k=ST, m=2)
                else:
                    dst = vsplit[:, :, 0:P]
                    src = ou[:, 0, :].rearrange("p (k d) -> p k d", k=ST)
                A(dst, src, ACT.Copy).then_inc(v_hi, 1)

            def output_copy(u):
                act.wait_ge(pv, u + 1)
                if u < MOBA_UNITS:
                    if u:
                        act.wait_ge(o_read, u)
                    A(o_tmp[0:HALF, :], ou[HALF:P, 0, :], ACT.Copy)
                    A(o_tmp[HALF:P, :], ou[0:HALF, 1, :], ACT.Copy).then_inc(o_half, 1)
                else:
                    if u > MOBA_UNITS:
                        act.wait_ge(o_bc, u - MOBA_UNITS)
                    A(o_tmp[:, :], ou[:, 0, :], ACT.Square).then_inc(o_sq, 1)
                    act.wait_ge(y_lo, u)
                    A(o_sb[:, :], ou[:, 0, :], ACT.Copy).then_inc(o_half, 1)

            def output_mean(u):
                act.wait_ge(o_ms, u - MOBA_UNITS + 1)
                A(rms4[:, :], ou[:, 1, 0:ST], ACT.Copy, scale=1.0 / P).then_inc(o_mean, 1)

            def z_gate(u):
                act.wait_ge(pj_read, 4 * u + Z + 1)
                if u:
                    act.wait_ge(z_done, u)
                A(ztanh, zbuf[:, u % 3, :], ACT.Tanh).then_inc(z_tanh, 1)

            def y_round(u):
                act.wait_ge(y_ready, u + 1)
                A(ysplit[:, 0, u, :], o_sb[:, :], ACT.Copy).then_inc(y_hi, 1)

            def embed_read(g):
                t, n = divmod(g, NH)
                act.wait_ge(pe_mm, g + 1)
                if g == 0:
                    act.wait_ge(qk_lo, NU)
                    act.wait_ge(pj_read, 4 * NU)
                A(pe[:, t, n * SEQ:(n + 1) * SEQ], pj[:, g % 2, :], ACT.Copy, scale=0.5).then_inc(pe_read, 1)

            def h_square(k):
                _, n, t = [x for x in ITEMS if x[0] == "out"][k]
                act.wait_ge(h_read, k + 1)
                if k:
                    act.wait_ge(h_sq, k)
                A(v_t[:, :], h[:, t, n * SEQ:(n + 1) * SEQ], ACT.Square, accum_out=ssq[:, t, n:n + 1]).then_inc(h_sq, 1)

            def h_turned_hi(k):
                i = [x for x in range(len(ITEMS)) if ITEMS[x][0] == "turn"][k]
                _, n, t = ITEMS[i]
                act.wait_ge(item, i + 1)
                A(usplit[:, 0, 4 * n:4 * n + 4, t * P:(t + 1) * P], banks[BANK[i]].rearrange("p (b c) -> p b c", b=4),
                  ACT.Copy).then_inc(ht_hi, 1)

            def gate_tanh(k):
                i = [x for x in range(len(ITEMS)) if ITEMS[x][0] == "gate"][k]
                t = ITEMS[i][2]
                act.wait_ge(item, i + 1)
                if k == 0:
                    act.wait_ge(h_rstd, 1)
                    act.wait_ge(y_lo, NU)
                if k >= 2:
                    act.wait_ge(g_add, k - 1)
                A((o_sb, o_tmp)[k % 2][:, :], banks[BANK[i]], ACT.Tanh, scale=hrs[:, t:t + 1]).then_inc(g_tanh, 1)

            def f_square(k):
                _, n, t = [x for x in ITEMS if x[0] == "gate"][k]
                act.wait_ge(g_add, k + 1)
                act.wait_ge(f_sq, k) if k else act.wait_ge(h_sq, ST * NH)
                A(v_t[:, :], h[:, t, n * SEQ:(n + 1) * SEQ], ACT.Square, accum_out=fsq[:, t, n:n + 1]).then_inc(f_sq, 1)

            act.dma_start(gm[:, :], g_mix).then_inc(gm_in, 16)
            for kt in (0, 2):
                act.dma_start(xt_raw[:, kt, :], x_t[kt * P:(kt + 1) * P, :]).then_inc(xt_in[kt], 16)

            act.wait_ge(gm_in, 16)
            for kt in range(KT):
                if kt % 2 == 0:
                    w = slice(128 * kt, 128 * kt + 256)
                    act.wait_ge(w0_in[kt // 2], 16)
                    A(wsplit[:, 0, 0, w], raw[:, 0, w], ACT.Copy).then_inc(w0_hi, 1)
                act.wait_ge(xt_in[kt], 16)
                A(usplit[:, 0, kt, :], xt_raw[:, kt, :], ACT.Copy, scale=gm[:, kt:kt + 1]).then_inc(u_hi, 1)
            weights_hi(1)
            for kt in range(0, KT, 2):
                act.wait_ge(u_lo, kt + 1)
                A(xt_raw[:, kt, :], xt_raw[:, kt, :], ACT.Square).then_inc(x_sq, 1)
            weights_hi(2)
            weights_hi(3)
            act.wait_ge(x_ms, 1)
            A(rms4[:, :], ou[:, 1, 0:ST], ACT.Copy, scale=1.0 / D_MODEL).then_inc(x_mean, 1)
            act.wait_ge(lam_sum, 1)
            A(lam_e[:, :], lam_s[:, :], ACT.Exp).then_inc(lam_exp, 1)
            act.wait_ge(x_bc, 1)
            A(rstd, ou[:, 1, :], ACT.Copy).then_inc(rstd_done, 1)

            for u in range(NU):
                if u >= 2:
                    probs_hi(u - 2, 1)
                if u:
                    weights_hi(4 * u + 3)
                if u >= 2:
                    probs_hi(u - 2, 2)
                if u >= 1:
                    exponentials(u - 1, 0)
                qk_hi_of(u, Q)
                if u >= 3:
                    y_round(u - 3)
                weights_hi(4 * u + 4)
                if u >= 1:
                    exponentials(u - 1, 1)
                if u >= 2:
                    output_copy(u - 2)
                z_gate(u)
                qk_hi_of(u, K)
                weights_hi(4 * u + 5)
                if u >= 1:
                    exponentials(u - 1, 2)
                if u >= 1:
                    probs_hi(u - 1, 0)
                if u - 2 >= MOBA_UNITS:
                    output_mean(u - 2)
                if u >= 1:
                    values_hi(u - 1)
                weights_hi(4 * u + 6)
            embed_read(0)
            embed_read(1)
            probs_hi(NU - 2, 1)
            embed_read(2)
            weights_hi(T_OUT)
            exponentials(NU - 1, 0)
            y_round(NU - 3)
            embed_read(3)
            probs_hi(NU - 2, 2)
            weights_hi(T_OUT + 1)
            embed_read(4)
            exponentials(NU - 1, 1)
            embed_read(5)
            output_copy(NU - 2)
            exponentials(NU - 1, 2)
            probs_hi(NU - 1, 0)
            embed_read(6)
            embed_read(7)
            output_mean(NU - 2)
            values_hi(NU - 1)
            weights_hi(T_OUT + 2)
            probs_hi(NU - 1, 1)
            weights_hi(T_OUT + 3)
            probs_hi(NU - 1, 2)
            y_round(NU - 2)
            output_copy(NU - 1)
            output_mean(NU - 1)
            weights_hi(T_OUT + 4)
            weights_hi(T_OUT + 5)
            y_round(NU - 1)
            for j in range(T_OUT + 6, T_GATE + KT // 2):
                weights_hi(j)
            for k in range(7):
                h_square(k)
            for k in (0, 1):
                h_turned_hi(k)
            h_square(7)
            for k in (2, 3):
                h_turned_hi(k)
            for j in range(T_GATE + KT // 2, T_ALL):
                weights_hi(j)
            gate_tanh(0)
            h_turned_hi(4), h_turned_hi(5)
            gate_tanh(1)
            h_turned_hi(6), h_turned_hi(7)
            for k in range(2, 2 * ST):
                f_square(k - 2)
                gate_tanh(k)
            f_square(2 * ST - 2)
            f_square(2 * ST - 1)

        @block.vector
        def _(dve):
            V_ = nc.vector

            def weights_lo(j):
                dve.wait_ge(w_hi, j)
                hi, lo = split_target(j)
                if j < T_GATE:
                    V_.tensor_tensor(lo, raw[:, j % RAW, :], hi.bitcast(f32), ALU.subtract).then_inc(w_lo, 1)
                else:
                    for k in range(2):
                        kt, c = 2 * ((j - T_GATE) % (KT // 2)) + k, slice(k * SEQ, (k + 1) * SEQ)
                        last = V_.scalar_tensor_tensor(lo[:, c], raw[:, j % RAW, c], gp[:, kt:kt + 1], hi[:, c].bitcast(f32),
                                                       ALU.mult, ALU.subtract)
                    last.then_inc(w_lo, 1)

            def rope_start(u, t):
                n = 2 * u + t
                dve.wait_ge(proj, 4 * u + t + 1)
                if u:
                    dve.wait_ge(roped, n - 1)
                    dve.wait_ge(qk_lo, n - 1)
                o = pj_bank(4 * u + t)
                V_.stream_shuffle(shuf[:, t, :], o, [*range(8, 16), *range(8), *range(16, 32)])
                V_.tensor_tensor(rot[:, t, :], o, rope_r[:, 0, :], ALU.mult).then_inc(pj_read, 1)

            def z_scale(u):
                dve.wait_ge(proj, 4 * u + Z + 1)
                if u >= 3:
                    dve.wait_ge(y_ready, u - 2)
                V_.scalar_tensor_tensor(zbuf[:, u % 3, :], pj_bank(4 * u + Z), 0.5, rstd, ALU.mult, ALU.mult).then_inc(pj_read, 1)

            def z_silu(u):
                dve.wait_ge(z_tanh, u + 1)
                V_.scalar_tensor_tensor(zbuf[:, u % 3, :], ztanh, 1.0, zbuf[:, u % 3, :], ALU.add, ALU.mult).then_inc(z_done, 1)

            def v_scale(u):
                dve.wait_ge(proj, 4 * u + V + 1)
                if u:
                    dve.wait_ge(vtrans, u)
                V_.tensor_tensor(v_t[:, :], pj_bank(4 * u + V), rstd, ALU.mult).then_inc(pj_read, 1)

            def maxima(u, step):
                n = 3 * u + step
                dve.wait_ge(scores, n + 1)
                d = sc[:, :, 0:SEQ].rearrange("p m (b c) -> p m b c", c=P)
                if step == 0:
                    for m in range(2):
                        last = V_.tensor_tensor(d[:, m, 0:3:2, :], d[:, m, 0:3:2, :], mask.unsqueeze(1).broadcast_to([P, 2, P]), ALU.add)
                    last.then_inc(masked, 1)
                else:
                    b = STEP_W[step] // P - 1
                    V_.tensor_tensor(d[:, :, b, :], d[:, :, b, :], mask.unsqueeze(1).broadcast_to([P, 2, P]), ALU.add).then_inc(masked, 1)
                dve.wait_ge(masked, n + 1)
                c = 0
                for q in STEP_TILES[step]:
                    last = V_.tensor_reduce(nmax[:, q, :], sc[:, :, c:c + (q + 1) * P], AX.X, ALU.max, negate=True)
                    c += (q + 1) * P
                last.then_inc(maxes, 1)

            def reciprocals(u, step):
                n, tiles = 3 * u + step, slice(STEP_TILES[step][0], STEP_TILES[step][-1] + 1)
                dve.wait_ge(exps, n + 1)
                if u:
                    dve.wait_ge(probs_ready, n - 2)
                V_.reciprocal(rinv[:, tiles, :], rsum[:, tiles, :]).then_inc(recips, 1)
                if u >= MOBA_UNITS:
                    k = n - STEPS * MOBA_UNITS
                    if k == 0:
                        dve.wait_ge(lam_done, 1)
                    dve.wait_ge(recips, n + 1 + k)
                    V_.tensor_scalar(rinv[:, tiles, 1:2], rinv[:, tiles, 1:2], nlam[:, 0:1], None, ALU.mult).then_inc(recips, 1)

            def combine(u, step):
                n = 3 * u + step
                dve.wait_ge(weighted, n - STEPS * MOBA_UNITS + 1)
                c = STEP_COL[step]
                for q in STEP_TILES[step]:
                    w = slice(c, c + (q + 1) * P)
                    last = V_.scalar_tensor_tensor(probs[:, 0, w], probs[:, 0, w], rinv[:, q, 0:1], probs[:, 1, w], ALU.mult, ALU.add)
                    c += (q + 1) * P
                last.then_inc(probs_ready, 1)

            def probs_lo(u, step):
                dve.wait_ge(p_hi, 3 * u + step + 1)
                moba = u < MOBA_UNITS
                for (src, dst), (_, hi) in zip(per_map(pt_views(pt_lo, step), moba), per_map(pt_views(pt_hi, step), moba)):
                    last = V_.tensor_tensor(dst, src, hi.bitcast(f32), ALU.subtract)
                last.then_inc(p_lo, 1)

            def qk_lo_of(u, t):
                dve.wait_ge(qk_hi, 2 * u + t + 1)
                V_.scalar_tensor_tensor(qksplit[:, t, 1, :], rot[:, t, :], (SCALE, 1.0)[t], qksplit[:, t, 0, :].bitcast(f32),
                                        ALU.mult, ALU.subtract).then_inc(qk_lo, 1)

            def values_lo(u):
                dve.wait_ge(v_hi, u + 1)
                if u < MOBA_UNITS:
                    v = vsplit[:, :, :].rearrange("p k (m i d) -> p k m i d", m=2, i=2)
                    src = ou[:, 0, :].rearrange("p (k m d) -> p k m d", k=ST, m=2)
                    for m in range(2):
                        last = V_.tensor_tensor(v[:, :, m, 1, :], src[:, :, m, :], v[:, :, m, 0, :].bitcast(f32), ALU.subtract)
                    last.then_inc(v_lo, 1)
                else:
                    src = ou[:, 0, :].rearrange("p (k d) -> p k d", k=ST)
                    V_.tensor_tensor(vsplit[:, :, P:2 * P], src, vsplit[:, :, 0:P].bitcast(f32), ALU.subtract).then_inc(v_lo, 1)

            def output_sum(u):
                dve.wait_ge(o_half, u + 1)
                if u:
                    dve.wait_ge(y_lo, u)
                V_.tensor_tensor(o_sb[0:HALF, :], ou[0:HALF, 0, :], o_tmp[0:HALF, :], ALU.add)
                V_.tensor_tensor(o_sb[HALF:P, :], ou[HALF:P, 1, :], o_tmp[HALF:P, :], ALU.add).then_inc(o_read, 1)

            def output_norm(u):
                k = u - MOBA_UNITS
                dve.wait_ge(o_bc, k + 1)
                if k == 0:
                    dve.wait_ge(gs_done, 1)
                dve.wait_ge(o_half, u + 1)
                V_.scalar_tensor_tensor(o_sb[:, :], o_sb[:, :], gs8[:, 0:1], ou[:, 1, :], ALU.mult, ALU.mult).then_inc(o_read, 1)

            def widen_rms(u):
                dve.wait_ge(o_rstd, u - MOBA_UNITS + 1)
                V_.tensor_copy(o_tmp[:, :].rearrange("p (t c) -> p t c", t=ST),
                               rms4[:, :].unsqueeze(2).broadcast_to([P, ST, P])).then_inc(o_wide, 1)

            def y_rest(u):
                dve.wait_ge(y_hi, u + 1)
                V_.tensor_tensor(ysplit[:, 1, u, :], o_sb[:, :], ysplit[:, 0, u, :].bitcast(f32), ALU.subtract).then_inc(y_lo, 1)

            def residual(k):
                i = [x for x in range(len(ITEMS)) if ITEMS[x][0] == "out"][k]
                _, n, t = ITEMS[i]
                dve.wait_ge(item, i + 1)
                if n == 0:
                    dve.wait_ge(x_in[t], 16)
                c = slice(n * SEQ, (n + 1) * SEQ)
                V_.tensor_tensor(h[:, t, c], banks[BANK[i]], h[:, t, c], ALU.add).then_inc(h_read, 1)

            def h_turned_lo(k):
                i = [x for x in range(len(ITEMS)) if ITEMS[x][0] == "turn"][k]
                _, n, t = ITEMS[i]
                dve.wait_ge(ht_hi, k + 1)
                a = (slice(None), slice(4 * n, 4 * n + 4), slice(t * P, (t + 1) * P))
                V_.tensor_tensor(usplit[:, 1, a[1], a[2]], banks[BANK[i]].rearrange("p (b c) -> p b c", b=4),
                                 usplit[:, 0, a[1], a[2]].bitcast(f32), ALU.subtract).then_inc(ht_lo, 1)

            def gate_add(k):
                _, n, t = [x for x in ITEMS if x[0] == "gate"][k]
                g, c = (o_sb, o_tmp)[k % 2][:, :], slice(n * SEQ, (n + 1) * SEQ)
                dve.wait_ge(g_tanh, k + 1)
                V_.scalar_tensor_tensor(g, g, 1.0, pe[:, t, c], ALU.add, ALU.mult).then_inc(g_mul, 1)
                dve.wait_ge(g_mul, k + 1)
                V_.tensor_tensor(h[:, t, c], h[:, t, c], g, ALU.add).then_inc(g_add, 1)

            def final_scale(t):
                dve.wait_ge(f_rstd, t + 1)
                V_.scalar_tensor_tensor(h[:, t, :], h[:, t, :], frs[:, t:t + 1], gfin[:, :], ALU.mult, ALU.mult).then_inc(f_out, 1)

            for kt in range(KT):
                if kt % 2 == 0:
                    w = slice(128 * kt, 128 * kt + 256)
                    dve.wait_ge(w0_hi, kt // 2 + 1)
                    V_.tensor_tensor(wsplit[:, 0, 1, w], raw[:, 0, w], wsplit[:, 0, 0, w].bitcast(f32), ALU.subtract).then_inc(w0_lo, 1)
                dve.wait_ge(u_hi, kt + 1)
                V_.scalar_tensor_tensor(usplit[:, 1, kt, :], xt_raw[:, kt, :], gm[:, kt:kt + 1], usplit[:, 0, kt, :].bitcast(f32),
                                        ALU.mult, ALU.subtract).then_inc(u_lo, 1)
            weights_lo(1)
            for kt in range(1, KT):
                dve.wait_ge(x_sq, kt // 2 + 1)
                dve.wait_ge(pool_own, (kt + 1) // 2)
                if kt > 1:
                    dve.wait_ge(x_sum, kt - 1)
                a = xt_raw[:, 0, :] if kt == 1 else xsum[:, :]
                V_.tensor_tensor(xsum[:, :], a, xt_raw[:, kt, :], ALU.add).then_inc(x_sum, 1)
            weights_lo(2)
            weights_lo(3)
            dve.wait_ge(small_in, 64)
            V_.tensor_tensor(lam_pr[:, :, :], lam_in[:, 0:3:2, :], lam_in[:, 1:4:2, :], ALU.mult).then_inc(lam_prod, 1)
            dve.wait_ge(lam_prod, 1)
            V_.tensor_reduce(lam_s[:, :], lam_pr[:, :, :], AX.X, ALU.add).then_inc(lam_sum, 1)
            V_.tensor_scalar(gs8[:, :], gs[:, :], 1.0 - LAMBDA_INIT, None, ALU.mult).then_inc(gs_done, 1)
            dve.wait_ge(x_rstd, 1)
            V_.tensor_copy(xsum[:, :].rearrange("p (t c) -> p t c", t=ST),
                           rms4[:, :].unsqueeze(2).broadcast_to([P, ST, P])).then_inc(x_wide, 1)
            dve.wait_ge(lam_exp, 1)
            V_.tensor_scalar(nlam[:, :], lam_e[:, 1:2], lam_e[:, 0:1], LAMBDA_INIT, ALU.subtract, ALU.subtract).then_inc(lam_done, 1)
            dve.wait_ge(rstd_done, 1)
            dve.wait_ge(rope_in, 16)
            for i in range(2):
                last = V_.tensor_tensor(rope_r[:, i, :], rope_r[:, i, :], rstd, ALU.mult)
            last.then_inc(tab_done, 1)
            dve.wait_ge(tab_done, 1)

            def inverses(u, step):
                reciprocals(u, step)
                if u >= MOBA_UNITS:
                    combine(u, step)

            for u in range(NU):
                if u >= 2:
                    probs_lo(u - 2, 1)
                if u - 3 >= MOBA_UNITS:
                    widen_rms(u - 3)
                rope_start(u, Q)
                if u:
                    weights_lo(4 * u + 3)
                rope_start(u, K)
                if u >= 1:
                    maxima(u - 1, 0)
                if u >= 2:
                    probs_lo(u - 2, 2)
                if u >= 1:
                    inverses(u - 1, 0)
                if u - 3 >= MOBA_UNITS:
                    output_norm(u - 3)
                qk_lo_of(u, Q)
                weights_lo(4 * u + 4)
                z_scale(u)
                if u >= 1:
                    maxima(u - 1, 1)
                if u >= 1:
                    inverses(u - 1, 1)
                if u >= 3:
                    y_rest(u - 3)
                if 0 <= u - 2 < MOBA_UNITS:
                    output_sum(u - 2)
                if u >= 1:
                    maxima(u - 1, 2)
                z_silu(u)
                qk_lo_of(u, K)
                v_scale(u)
                weights_lo(4 * u + 5)
                if u >= 1:
                    probs_lo(u - 1, 0)
                if u >= 1:
                    values_lo(u - 1)
                if u >= 1:
                    inverses(u - 1, 2)
                weights_lo(4 * u + 6)
            probs_lo(NU - 2, 1)
            widen_rms(NU - 3)
            output_norm(NU - 3)
            weights_lo(T_OUT)
            maxima(NU - 1, 0)
            inverses(NU - 1, 0)
            probs_lo(NU - 2, 2)
            weights_lo(T_OUT + 1)
            y_rest(NU - 3)
            maxima(NU - 1, 1)
            inverses(NU - 1, 1)
            maxima(NU - 1, 2)
            probs_lo(NU - 1, 0)
            inverses(NU - 1, 2)
            values_lo(NU - 1)
            weights_lo(T_OUT + 2)
            probs_lo(NU - 1, 1)
            widen_rms(NU - 2)
            weights_lo(T_OUT + 3)
            probs_lo(NU - 1, 2)
            output_norm(NU - 2)
            y_rest(NU - 2)
            widen_rms(NU - 1)
            output_norm(NU - 1)
            weights_lo(T_OUT + 4)
            weights_lo(T_OUT + 5)
            y_rest(NU - 1)
            for j in range(T_OUT + 6, T_GATE):
                weights_lo(j)
            for k in range(4):
                residual(k)
            for j in range(T_GATE, T_GATE + KT // 2):
                weights_lo(j)
            for k in range(4, 7):
                residual(k)
            h_turned_lo(0), h_turned_lo(1)
            residual(7)
            h_turned_lo(2), h_turned_lo(3)
            for j in range(T_GATE + KT // 2, T_ALL):
                weights_lo(j)
            h_turned_lo(4), h_turned_lo(5)
            gate_add(0)
            h_turned_lo(6), h_turned_lo(7)
            for k in range(1, 2 * ST):
                gate_add(k)
                if k > ST:
                    final_scale(k - ST - 1)
            final_scale(ST - 1)

        @block.gpsimd
        def _(pool):
            G = nc.gpsimd
            own = [0]

            def link(ins):
                own[0] += 1
                ins.then_inc(pool_own, 1)
                pool.wait_ge(pool_own, own[0])

            def rope_finish(u, t):
                pool.wait_ge(pj_read, 4 * u + t + 1)
                pool.wait_ge(tab_done, 1)
                link(G.tensor_tensor(shuf[:, t, :], shuf[:, t, :], rope_r[:, 1, :], ALU.mult))
                G.tensor_tensor(rot[:, t, :], rot[:, t, :], shuf[:, t, :], ALU.add).then_inc(roped, 1)

            def normalise(u, step):
                n = 3 * u + step
                moba = u < MOBA_UNITS
                pool.wait_ge(recips, n + 1 if moba else 2 * n + 2 - STEPS * MOBA_UNITS)
                c = STEP_COL[step]
                for q in STEP_TILES[step]:
                    w = slice(c, c + (q + 1) * P)
                    for m in (0, 1) if moba else (1,):
                        last = G.tensor_scalar(probs[:, m, w], probs[:, m, w], rinv[:, q, m:m + 1], 1.0, ALU.mult, ALU.mult)
                    c += (q + 1) * P
                last.then_inc(probs_ready if moba else weighted, 1)

            def gate_output(u):
                pool.wait_ge(o_read, u + 1)
                pool.wait_ge(z_done, u + 1)
                G.tensor_tensor(o_sb[:, :], o_sb[:, :], zbuf[:, u % 3, :], ALU.mult).then_inc(y_ready, 1)

            def inverse_rms(to, a, b, tmp, done, half):
                link(G.tensor_tensor(tmp, a, b, ALU.add))
                link(G.tensor_scalar(tmp, tmp, 1.0 / D_MODEL, EPS, ALU.mult, ALU.add))
                if half:
                    link(G.tensor_tensor(tmp, tmp, mhalf[:, 0:tmp.shape[1]], ALU.pow))
                    G.tensor_scalar(to, tmp, 0.5, 1.0, ALU.mult, ALU.mult).then_inc(done, 1)
                else:
                    G.tensor_tensor(to, tmp, mhalf[:, 0:tmp.shape[1]], ALU.pow).then_inc(done, 1)

            for kt in range(1, KT, 2):
                pool.wait_ge(u_lo, kt + 1)
                own[0] += 1
                G.tensor_tensor(xt_raw[:, kt, :], xt_raw[:, kt, :], xt_raw[:, kt, :], ALU.mult).then_inc(pool_own, 1)
            link(G.memset(mhalf[:, :], -0.5))

            def token_rms(mean_done, count, done):
                pool.wait_ge(mean_done, count)
                link(G.tensor_scalar(rms4[:, :], rms4[:, :], 1.0, EPS, ALU.mult, ALU.add))
                G.tensor_tensor(rms4[:, :], rms4[:, :], mhalf[:, :], ALU.pow).then_inc(done, 1)

            token_rms(x_mean, 1, x_rstd)
            for u in range(NU + 2):
                if u - 3 >= MOBA_UNITS:
                    token_rms(o_mean, u - 3 - MOBA_UNITS + 1, o_rstd)
                if u < NU:
                    rope_finish(u, Q)
                if 1 <= u <= NU:
                    normalise(u - 1, 0)
                if u >= 3:
                    gate_output(u - 3)
                if u < NU:
                    rope_finish(u, K)
                if 1 <= u <= NU:
                    normalise(u - 1, 1)
                if 1 <= u <= NU:
                    normalise(u - 1, 2)
            token_rms(o_mean, NU - MOBA_UNITS, o_rstd)
            gate_output(NU - 1)
            pool.wait_ge(h_sq, ST * NH)
            inverse_rms(hrs[:, :], ssq[:, :, 0], ssq[:, :, 1], ssa[:, :], h_rstd, True)
            for t in range(ST):
                pool.wait_ge(f_sq, ST + t + 1)
                inverse_rms(frs[:, t:t + 1], fsq[:, t, 0:1], fsq[:, t, 1:2], fsa[:, t:t + 1], f_rstd, False)


def kernel(**inputs):
    import concourse.bacc as bacc
    from concourse.bass_utils import run_bass_kernel_spmd as run

    a = {k: np.asarray(v) for k, v in inputs.items()}
    units = D_MODEL // P
    starts = []
    for u in range(units):
        part, q = (0, u) if u < units // 2 else (3, u - units // 2)
        starts += [(part + i) * 512 + q * P for i in (0, 1)] + [3072 + u * P, (part + 2) * 512 + q * P]
    w = a["w_in"][0].reshape(D_MODEL // P, P, -1)
    w_in = np.stack([w[:, :, c:c + P] for c in starts])
    w_in = w_in.reshape(units, 4, D_MODEL // P, P, P).transpose(0, 3, 1, 2, 4)

    inv = np.float32(ROPE_THETA) ** (-np.arange(0, ROPE_DIM, 2, dtype=np.float32) / np.float32(ROPE_DIM))
    ang = inv[:, None] * np.arange(SEQ, dtype=np.float32)[None, :]
    rope = np.zeros((2, P, SEQ), np.float32)
    rope[0] = 1.0
    for b in range(0, P, HEAD_DIM):
        rope[0, b:b + ROPE_DIM] = np.tile(np.cos(ang), (2, 1))
        rope[1, b:b + ROPE_DIM] = np.concatenate([-np.sin(ang), np.sin(ang)])
    consts = np.concatenate([np.eye(P), np.where(np.tri(P) > 0, 0.0, -3e38), np.ones((P, P))], 1).astype(np.float32)

    arrays = {
        "x_t": a["x"][0].T, "x": a["x"][0], "p_t": a["p"][0, 0].T,
        "w_in": w_in.reshape(units, P, 4, D_MODEL), "w_out": a["w_out"][0], "w_gate": a["w_ple_gate"][0], "w_ple": a["w_ple"][0],
        "g_mix": a["g_mix"][0].reshape(-1, P).T, "g_ple": a["g_ple"][0].reshape(-1, P).T,
        "g_subln": a["g_subln"][0].reshape(P, 1), "g_final": a["g_final"],
        "lams": np.stack([a[n][0] for n in ("diff_lq1", "diff_lk1", "diff_lq2", "diff_lk2")]),
        "rope": rope, "consts": consts,
    }
    arrays = {f"in_{k}": np.ascontiguousarray(v) for k, v in arrays.items()}
    nc = bacc.Bacc("TRN2", target_bir_lowering=False, num_devices=1)
    args = [nc.dram_tensor(k, v.shape, mybir.dt.from_np(v.dtype), kind="ExternalInput").ap() for k, v in arrays.items()]
    out = nc.dram_tensor("out", (SEQ, D_MODEL), mybir.dt.float32, kind="ExternalOutput").ap()
    build_program(nc, *args, out)
    r = run(nc, [arrays], core_ids=[0])
    return r.results[0]["out"].reshape(1, SEQ, D_MODEL)
```

```python
import numpy as np
import concourse.bass as bass
from concourse import mybir
from concourse.alu_op_type import AluOpType as ALU
from contextlib import ExitStack

D_MODEL, SEQ, PLE_DIM, HEAD_DIM = 1024, 512, 256, 64
MOBA_HEADS, MOBA_BLOCK, MOBA_TOPK, DIFF_HEADS = 8, 256, 3, 4
ROPE_THETA, ROPE_DIM = 500000.0, 16
EPS = 1e-6
LAMBDA_INIT = 0.8 - 0.6 * 1.0
P = 128
assert min(MOBA_TOPK, SEQ // MOBA_BLOCK) == SEQ // MOBA_BLOCK


def build_program(nc, x_t, x, p_t, w_in, w_out, w_gate, w_ple, g_mix, g_ple, g_subln, g_final, lams,
                  rope, consts, out):
    f32, f32r = mybir.dt.float32, mybir.dt.float32r
    ACT = mybir.ActivationFunctionType
    AX = mybir.AxisListType

    KT = D_MODEL // P
    ST = SEQ // P
    NU = D_MODEL // P
    MOBA_UNITS = MOBA_HEADS * HEAD_DIM // P
    NH = D_MODEL // SEQ
    HALF = HEAD_DIM
    Q, K, Z, V = range(4)
    STEPS = 3
    STEP_TILES = [(0, 1), (2,), (3,)]
    STEP_COL = [0, 384, 768]
    STEP_W = [384, 384, 512]
    PT_BLOCKS = 12
    SCALE = float(HEAD_DIM) ** -0.5

    T_IN = 0
    T_PLE = T_IN + 4 * NU
    T_P = T_PLE + 2
    T_OUT = T_P + 1
    T_GATE = T_OUT + NH * KT // 2
    T_ALL = T_GATE + NH * KT // 2
    RAW = 4

    ctx = ExitStack()
    with ctx:
        def sb(name, shape, dt=f32):
            return ctx.enter_context(nc.sbuf_tensor(name, shape, dt))

        def sem(name):
            return ctx.enter_context(nc.semaphore(name))

        wsplit = sb("wsplit", [P, 4, 2, 1024], f32r)
        usplit = sb("usplit", [P, 2, KT, SEQ], f32r)
        csplit = sb("csplit", [P, 9216], f32r)
        ysplit = sb("ysplit", [P, 2, NU, SEQ], f32r)
        qksplit = sb("qksplit", [P, 2, 2, SEQ], f32r)
        vsplit = sb("vsplit", [P, ST, 2 * P], f32r)
        pt_hi = csplit[:, 0:3072].rearrange("p (m c) -> p m c", m=2)
        pt_lo = csplit[:, 3072:6144].rearrange("p (m c) -> p m c", m=2)
        qs = csplit[:, 6144:7168].rearrange("p (m c) -> p m c", m=2)
        kst = csplit[:, 7168:9216].rearrange("p (i m c) -> p i m c", i=2, m=2)
        k_hi = csplit[:, 7168:8192].rearrange("p (m c) -> p m c", m=2)
        k_lo = csplit[:, 8192:9216].rearrange("p (m c) -> p m c", m=2)
        wout_n = [usplit[:, :, :, :].rearrange("p s k c -> p (s k c)"),
                  wsplit[:, :, :, :].rearrange("p a s c -> p (a s c)")]
        wgate_n = [csplit[:, 0:8192], wsplit[:, :, :, :].rearrange("p a s c -> p (a s c)")]

        def chunk(region, c):
            v = region.rearrange("p (c s n) -> p c s n", c=KT // 2, s=2)
            return v[:, c, 0, :], v[:, c, 1, :]

        def chunk_tile(region, kt):
            hi, lo = chunk(region, kt // 2)
            o = (kt % 2) * SEQ
            return hi[:, o:o + SEQ], lo[:, o:o + SEQ]

        raw = sb("raw", [P, RAW, 1024])
        hbuf = sb("hbuf", [P, 4096])
        tbuf = sb("tbuf", [P, 4096])
        xt_raw = hbuf[:, :].rearrange("p (k c) -> p k c", k=KT)
        probs = hbuf[:, 0:2560].rearrange("p (m c) -> p m c", m=2)
        zbuf = hbuf[:, 2560:4096].rearrange("p (b c) -> p b c", b=3)
        h = hbuf[:, :].rearrange("p (s d) -> p s d", s=ST)
        shuf = tbuf[:, 0:1024].rearrange("p (b c) -> p b c", b=2)
        rot = tbuf[:, 1024:2048].rearrange("p (b c) -> p b c", b=2)
        rope_r = tbuf[:, 2048:3072].rearrange("p (b c) -> p b c", b=2)
        rstd = tbuf[:, 3072:3584]
        ztanh = tbuf[:, 3584:4096]
        pe = tbuf[:, :].rearrange("p (s d) -> p s d", s=ST)
        v_t = sb("v_t", [P, SEQ])
        o_sb = sb("o_sb", [P, SEQ])
        o_tmp = sb("o_tmp", [P, SEQ])
        xsum = sb("xsum", [P, SEQ])
        gfin = sb("gfin", [P, D_MODEL])
        cst = sb("cst", [P, 3 * P])
        ident, mask, ones = cst[:, 0:P], cst[:, P:2 * P], cst[:, 2 * P:3 * P]
        gm = sb("gm", [P, KT])
        gp = sb("gp", [P, KT])
        gs = sb("gs", [P, 1])
        gs8 = sb("gs8", [P, 1])
        lam_in = sb("lam_in", [P, 4, HEAD_DIM])
        lam_pr = sb("lam_pr", [P, 2, HEAD_DIM])
        lam_s = sb("lam_s", [P, 2])
        lam_e = sb("lam_e", [P, 2])
        nlam = sb("nlam", [P, 1])
        rms4 = sb("rms4", [P, ST])
        mhalf = sb("mhalf", [P, ST])
        nmax = sb("nmax", [P, ST, 2])
        rsum = sb("rsum", [P, ST, 2])
        rinv = sb("rinv", [P, ST, 2])
        ssq = sb("ssq", [P, ST, 2])
        ssa = sb("ssa", [P, ST])
        hrs = sb("hrs", [P, ST])
        fsq = sb("fsq", [P, ST, 3])
        fsa = sb("fsa", [P, ST])
        frs = sb("frs", [P, ST])

        def ps(name):
            return ctx.enter_context(nc.psum_tensor(name, [P, 2, SEQ], f32))

        pj, sc, tr, ou = ps("pj"), ps("sc"), ps("tr"), ps("ou")
        banks = [pj[:, 0, :], pj[:, 1, :], sc[:, 0, :], sc[:, 1, :],
                 tr[:, 0, :], tr[:, 1, :], ou[:, 0, :], ou[:, 1, :]]

        raw_in = [sem(f"raw_in{i}") for i in range(RAW)]
        w0_in = [sem(f"w0_in{i}") for i in range(4)]
        xt_in = [sem(f"xt_in{k}") for k in range(KT)]
        x_in = [sem(f"x_in{t}") for t in range(ST)]
        gm_in, w0_hi, w0_lo, small_in, cst_in, rope_in, stored = [sem(n) for n in "gm_in w0_hi w0_lo small_in cst_in rope_in stored".split()]
        u_hi, u_lo, x_sq, x_sum, x_ms, x_mean, x_rstd, x_wide, x_bc, rstd_done, tab_done = [
            sem(n) for n in "u_hi u_lo x_sq x_sum x_ms x_mean x_rstd x_wide x_bc rstd_done tab_done".split()]
        lam_prod, lam_sum, lam_exp, lam_done, gs_done = [
            sem(n) for n in "lam_prod lam_sum lam_exp lam_done gs_done".split()]
        w_hi, w_lo, proj, pj_read, roped, qk_hi, qk_lo, stacked = [
            sem(n) for n in "w_hi w_lo proj pj_read roped qk_hi qk_lo stacked".split()]
        scores, masked, maxes, exps, recips, weighted, probs_ready, ptrans, p_hi, p_lo = [
            sem(n) for n in "scores masked maxes exps recips weighted probs_ready ptrans p_hi p_lo".split()]
        vtrans, v_hi, v_lo, pv, o_half, o_read, o_sq, o_ms, o_mean, o_rstd, o_wide, o_bc = [
            sem(n) for n in "vtrans v_hi v_lo pv o_half o_read o_sq o_ms o_mean o_rstd o_wide o_bc".split()]
        z_tanh, z_done, y_ready, y_hi, y_lo = [sem(n) for n in "z_tanh z_done y_ready y_hi y_lo".split()]
        pe_mm, pe_read, item, h_read, h_sq, h_rstd, ht_hi, ht_lo = [
            sem(n) for n in "pe_mm pe_read item h_read h_sq h_rstd ht_hi ht_lo".split()]
        g_tanh, g_mul, g_add, f_sq, f_gain, f_rstd, f_low, f_high, pool_own = [
            sem(n) for n in "g_tanh g_mul g_add f_sq f_gain f_rstd f_low f_high pool_own".split()]

        def pj_bank(j):
            return sc[:, j - 2, :] if j in (Z, V) else pj[:, j % 2, :]

        def split_target(j):
            if j < T_OUT:
                return wsplit[:, j % 4, 0, :], wsplit[:, j % 4, 1, :]
            t, region = (j - T_OUT, wout_n) if j < T_GATE else (j - T_GATE, wgate_n)
            return chunk(region[t // (KT // 2)], t % (KT // 2))

        def pt_blocks(step):
            return [[(0, 0, 1, 2), (2, 5, 1, 1)], [(0, 2, 4, 3)], [(0, 3, 4, 3), (3, 8, 1, 1)]][step]

        def pt_views(store, step):
            for first, to, stride, n in pt_blocks(step):
                src = tr[:, :, first * P:(first + n) * P].rearrange("p m (b c) -> p m b c", b=n)
                dst = store.rearrange("p m (b c) -> p m b c", c=P)[:, :, to:to + stride * (n - 1) + 1:stride, :]
                yield src, dst

        def per_map(pairs, moba):
            for src, dst in pairs:
                for m in range(2 if moba else 1):
                    yield src[:, m], dst[:, m]

        ITEMS = ([("out", 0, t) for t in range(ST)] + [("out", 1, 0), ("out", 1, 1), ("out", 1, 2), ("turn", 0, 0), ("turn", 1, 0),
                 ("out", 1, 3), ("turn", 0, 1), ("turn", 1, 1), ("gate", 0, 0), ("turn", 0, 2), ("turn", 1, 2), ("gate", 0, 1),
                 ("turn", 0, 3), ("turn", 1, 3), ("gate", 0, 2), ("gate", 0, 3)] + [("gate", 1, t) for t in range(ST)]
                 + [("gate", 1, ST - 1)])
        BANK = list(range(7)) + [(0, 1, 7, 2, 3, 4, 5, 6)[i % 8] for i in range(len(ITEMS) - 7)]

        GATES = [k for k in range(len(ITEMS)) if ITEMS[k][0] == "gate"]

        def item_cols(i):
            return slice(0, SEQ // 2) if i == len(ITEMS) - 2 else slice(SEQ // 2, SEQ) if i == len(ITEMS) - 1 else slice(0, SEQ)

        def gate_part(k):
            i = GATES[k]
            _, n, t = ITEMS[i]
            c = item_cols(i)
            return i, n, t, banks[BANK[i]][:, 0:c.stop - c.start], slice(n * SEQ + c.start, n * SEQ + c.stop)

        def nth(i):
            return sum(k[0] == ITEMS[i][0] for k in ITEMS[:i + 1])

        def number(kind, n, t):
            return ITEMS.index((kind, n, t))

        block = ctx.enter_context(nc.Block())

        @block.sync
        def _(sp):
            def load_tile(j):
                if j in (RAW, RAW + 1):
                    sp.wait_ge(w0_lo, 4)
                elif j > RAW:
                    sp.wait_ge(w_lo, j - RAW - 1)
                dst, halves = raw[:, j % RAW, :], raw[:, j % RAW, :].rearrange("p (k c) -> p k c", k=2)
                if j < T_PLE:
                    src = w_in[j // 4, :, j % 4, :]
                elif j < T_P:
                    src = w_ple[(j - T_PLE) * P:(j - T_PLE + 1) * P, :]
                elif j < T_OUT:
                    dst, src = halves, p_t.rearrange("(k p) c -> p k c", k=2)
                else:
                    w, t = (w_out, j - T_OUT) if j < T_GATE else (w_gate, j - T_GATE)
                    n, c = divmod(t, KT // 2)
                    dst = halves
                    src = w[2 * c * P:(2 * c + 2) * P, n * SEQ:(n + 1) * SEQ].rearrange("(k p) c -> p k c", k=2)
                sp.dma_start(dst, src).then_inc(raw_in[j % RAW], 16)

            def stack_qk(u):
                sp.wait_ge(qk_lo, 2 * u + 2)
                if u:
                    sp.wait_ge(scores, 3 * u)
                for m in range(2):
                    a = slice(m * HALF, (m + 1) * HALF)
                    for i in range(2):
                        to = slice(i * HALF, (i + 1) * HALF)
                        sp.dma_start(qs[to, m, :].bitcast(f32), qksplit[a, 0, i, :].bitcast(f32)).then_inc(stacked, 16)
                        sp.dma_start(kst[to, :, m, :].bitcast(f32), qksplit[a, 1, :, :].bitcast(f32)).then_inc(stacked, 16)

            for c in range(4):
                w = slice(256 * c, 256 * c + 256)
                sp.dma_start(raw[:, 0:2, w], w_in[0, :, 0:2, w]).then_inc(w0_in[c], 16)
                for k in (1,) if c == 0 else (3,) if c == 1 else (2 * c, 2 * c + 1):
                    sp.dma_start(xt_raw[:, k, :], x_t[k * P:(k + 1) * P, :]).then_inc(xt_in[k], 16)
            sp.dma_start(cst[:, :], consts).then_inc(cst_in, 16)
            load_tile(2), load_tile(3)
            sp.dma_start(rope_r, rope.rearrange("b p c -> p b c")).then_inc(rope_in, 16)
            sp.dma_start(lam_in[:, :, :], lams.partition_broadcast(P)).then_inc(small_in, 16)
            sp.dma_start(gp[:, :], g_ple).then_inc(small_in, 16)
            sp.dma_start(gs[:, :], g_subln).then_inc(small_in, 16)
            sp.dma_start(gfin[:, :], g_final.partition_broadcast(P)).then_inc(small_in, 16)
            for j in range(4, 8):
                load_tile(j)
            for u in range(NU):
                load_tile(4 * u + 8)
                stack_qk(u)
                load_tile(4 * u + 9)
                load_tile(4 * u + 10)
                load_tile(4 * u + 11)
            for j in range(4 * NU + 8, T_GATE):
                load_tile(j)
            sp.wait_ge(y_ready, NU)
            for t in range(ST):
                sp.dma_start(h[:, t, :], x[t * P:(t + 1) * P, :]).then_inc(x_in[t], 16)
            for j in range(T_GATE, T_ALL):
                load_tile(j)
            for t in range(ST):
                for done, c in ((f_high, slice(SEQ, D_MODEL)), (f_low, slice(0, SEQ))):
                    sp.wait_ge(done, t + 1)
                    sp.dma_start(out[t * P:(t + 1) * P, c], h[:, t, c]).then_inc(stored, 16)
            sp.wait_ge(stored, 2 * 16 * ST)

        @block.tensor
        def _(pe_eng):
            mm = nc.tensor.matmul

            def project(u, t, kts):
                j = 4 * u + t
                if kts[0] == 0:
                    pe_eng.wait_ge(w_lo, j - 1)
                if j >= 4 and kts[0] == 0:
                    pe_eng.wait_ge(pj_read, max(j - 1, 4) if j > 5 else j - 3)
                o = pj_bank(j)
                for kt in kts:
                    w_h, w_l = (wsplit[:, j % 4, i, kt * P:(kt + 1) * P] for i in range(2))
                    mm(o, w_h, usplit[:, 0, kt, :], start=kt == 0, stop=False)
                    mm(o, w_h, usplit[:, 1, kt, :], start=False, stop=False)
                    last = mm(o, w_l, usplit[:, 0, kt, :], start=False, stop=kt == KT - 1)
                if kts[-1] == KT - 1:
                    last.then_inc(proj, 1)

            def project_first():
                for kt in range(KT):
                    pe_eng.wait_ge(w0_lo, kt // 2 + 1)
                    pe_eng.wait_ge(u_lo, kt + 1)
                    for t in (Q, K):
                        w_h, w_l = (wsplit[:, t, i, kt * P:(kt + 1) * P] for i in range(2))
                        mm(pj[:, t, :], w_h, usplit[:, 0, kt, :], start=kt == 0, stop=False)
                        mm(pj[:, t, :], w_h, usplit[:, 1, kt, :], start=False, stop=False)
                        last = mm(pj[:, t, :], w_l, usplit[:, 0, kt, :], start=False, stop=kt == KT - 1)
                        if kt == KT - 1:
                            last.then_inc(proj, 1)

            def score(u, step):
                if step == 0:
                    pe_eng.wait_ge(stacked, 128 * (u + 1))
                    if u == 0:
                        pe_eng.wait_ge(pj_read, 4)
                if 3 * u + step:
                    pe_eng.wait_ge(exps, 3 * u + step)
                for m in range(2):
                    c = 0
                    for q in STEP_TILES[step]:
                        n = (q + 1) * P
                        o, w = sc[:, m, c:c + n], qs[:, m, q * P:(q + 1) * P]
                        mm(o, w, k_hi[:, m, 0:n], start=True, stop=False)
                        last = mm(o, w, k_lo[:, m, 0:n], start=False, stop=True)
                        c += n
                last.then_inc(scores, 1)

            def turn_probs(u, step):
                n = 3 * u + step
                pe_eng.wait_ge(probs_ready, n + 1)
                if n:
                    pe_eng.wait_ge(p_lo, n)
                for m in range(2 if u < MOBA_UNITS else 1):
                    for b in range(STEP_W[step] // P):
                        c = STEP_COL[step] + b * P
                        last = nc.tensor.transpose(tr[:, m, b * P:(b + 1) * P], probs[:, m, c:c + P], ident)
                last.then_inc(ptrans, 1)

            def turn_values(u):
                pe_eng.wait_ge(pj_read, 4 * u + V + 1)
                if u:
                    if u - 1 < MOBA_UNITS:
                        pe_eng.wait_ge(o_read, u)
                    else:
                        pe_eng.wait_ge(o_half, u)
                for kt in range(ST):
                    last = nc.tensor.transpose(ou[:, 0, kt * P:(kt + 1) * P], v_t[:, kt * P:(kt + 1) * P], ident)
                last.then_inc(vtrans, 1)

            def weigh_values(u):
                pe_eng.wait_ge(v_lo, u + 1)
                pe_eng.wait_ge(p_lo, 3 * u + 3)
                if u:
                    pe_eng.wait_ge(o_read, u)
                moba = u < MOBA_UNITS
                for m in range(2 if moba else 1):
                    for kt in range(ST):
                        b, n = (5 * kt if kt < 3 else 8) * P, (ST - kt) * P
                        o = ou[:, m, kt * P:SEQ]
                        ph, pl = pt_hi[:, m, b:b + n], pt_lo[:, m, b:b + n]
                        first, end = kt == 0, kt == ST - 1
                        if moba:
                            v = vsplit[:, kt, m * P:(m + 1) * P]
                            mm(o, v, ph, start=first, stop=False)
                            last = mm(o, v, pl, start=False, stop=end)
                        else:
                            mm(o, vsplit[:, kt, 0:P], ph, start=first, stop=False)
                            mm(o, vsplit[:, kt, 0:P], pl, start=False, stop=False)
                            last = mm(o, vsplit[:, kt, P:2 * P], ph, start=False, stop=end)
                last.then_inc(pv, 1)

            def sums_by_token(src, done):
                for t in range(ST):
                    last = mm(ou[:, 1, t:t + 1], src[:, t * P:(t + 1) * P], ones[:, 0:1], start=t == 0, stop=t == ST - 1,
                              skip_group_check=True)
                last.then_inc(done, 1)

            def to_all_partitions(src, done):
                for t in range(ST):
                    last = nc.tensor.transpose(ou[:, 1, t * P:(t + 1) * P], src[:, t * P:(t + 1) * P], ident)
                last.then_inc(done, 1)

            def square_sum(u):
                pe_eng.wait_ge(o_sq, u - MOBA_UNITS + 1)
                sums_by_token(o_tmp, o_ms)

            def spread_rms(u):
                pe_eng.wait_ge(o_wide, u - MOBA_UNITS + 1)
                to_all_partitions(o_tmp, o_bc)

            def embed(g):
                t, n = divmod(g, NH)
                if g == 0:
                    pe_eng.wait_ge(w_lo, T_OUT - 2)
                if g < 2:
                    pe_eng.wait_ge(pj_read, 4 * NU - 1 + g)
                else:
                    pe_eng.wait_ge(pe_read, g - 1)
                o = pj[:, g % 2, :]
                for kt in range(2):
                    p_h, p_l = (wsplit[:, 2, i, kt * SEQ + t * P:kt * SEQ + (t + 1) * P] for i in range(2))
                    w_h, w_l = (wsplit[:, kt, i, n * SEQ:(n + 1) * SEQ] for i in range(2))
                    mm(o, p_h, w_h, start=kt == 0, stop=False)
                    mm(o, p_h, w_l, start=False, stop=False)
                    last = mm(o, p_l, w_h, start=False, stop=kt == 1)
                last.then_inc(pe_mm, 1)

            def bank_free(i):
                before = [k for k in range(i) if BANK[k] == BANK[i]]
                if before:
                    b = before[-1]
                    pe_eng.wait_ge({"out": h_read, "turn": ht_lo, "gate": g_tanh}[ITEMS[b][0]], nth(b))
                elif BANK[i] < 2:
                    pe_eng.wait_ge(pe_read, ST * NH - 1 + BANK[i])
                elif BANK[i] < 4:
                    pe_eng.wait_ge(exps, STEPS * NU)
                elif BANK[i] < 6:
                    pe_eng.wait_ge(p_lo, STEPS * NU)
                else:
                    pe_eng.wait_ge(o_read, NU)

            def accumulate(i, left, region, kts):
                t, c = ITEMS[i][2], item_cols(i)
                o = banks[BANK[i]][:, 0:c.stop - c.start]
                for kt in kts:
                    a_h, a_l = (left[:, k, kt, t * P:(t + 1) * P] for k in range(2))
                    w_h, w_l = (w[:, c] for w in chunk_tile(region, kt))
                    mm(o, a_h, w_h, start=kt == 0, stop=False)
                    mm(o, a_h, w_l, start=False, stop=False)
                    last = mm(o, a_l, w_h, start=False, stop=kt == KT - 1)
                if kts[-1] == KT - 1:
                    last.then_inc(item, 1)

            def mix_out(i, kts):
                n = ITEMS[i][1]
                if kts[0] == 0:
                    bank_free(i)
                pe_eng.wait_ge(w_lo, T_OUT + n * KT // 2 + kts[-1] // 2 - 1)
                pe_eng.wait_ge(y_lo, kts[-1] + 1)
                accumulate(i, ysplit, wout_n[n], kts)

            def turn_h(i):
                _, n, t = ITEMS[i]
                bank_free(i)
                pe_eng.wait_ge(h_read, nth(number("out", n, t)))
                for b in range(4):
                    c = n * SEQ + b * P
                    last = nc.tensor.transpose(banks[BANK[i]][:, b * P:(b + 1) * P], h[:, t, c:c + P], ident)
                last.then_inc(item, 1)

            def gate(i):
                _, n, t = ITEMS[i]
                bank_free(i)
                pe_eng.wait_ge(w_lo, T_GATE + (n + 1) * KT // 2 - 2)
                pe_eng.wait_ge(ht_lo, nth(number("turn", 1, t)))
                accumulate(i, usplit, wgate_n[n], range(KT))

            lower, upper = range(KT // 2), range(KT // 2, KT)
            project_first()
            for u in range(NU - 1):
                if u:
                    project(u, Q, lower)
                    project(u, Q, upper)
                if u >= 2:
                    turn_probs(u - 2, 1)
                if u:
                    project(u, K, lower)
                if u - 3 >= MOBA_UNITS:
                    spread_rms(u - 3)
                if u:
                    project(u, K, upper)
                if u >= 2:
                    turn_probs(u - 2, 2)
                if u >= 1:
                    score(u - 1, 0)
                if u == 0:
                    pe_eng.wait_ge(cst_in, 16)
                    pe_eng.wait_ge(x_sum, KT - 1)
                    sums_by_token(xsum, x_ms)
                project(u, Z, lower)
                if u == 0:
                    pe_eng.wait_ge(x_wide, 1)
                    to_all_partitions(xsum, x_bc)
                project(u, Z, upper)
                if u >= 1:
                    score(u - 1, 1)
                project(u, V, lower)
                if u >= 2:
                    weigh_values(u - 2)
                project(u, V, upper)
                if u >= 1:
                    score(u - 1, 2)
                    turn_probs(u - 1, 0)
                if u - 2 >= MOBA_UNITS:
                    square_sum(u - 2)
                if u >= 1:
                    turn_values(u - 1)
            project(NU - 1, Q, lower)
            project(NU - 1, Q, upper)
            turn_probs(NU - 3, 1)
            project(NU - 1, K, lower)
            project(NU - 1, K, upper)
            spread_rms(NU - 4)
            score(NU - 2, 0)
            turn_probs(NU - 3, 2)
            project(NU - 1, Z, lower)
            project(NU - 1, Z, upper)
            score(NU - 2, 1)
            project(NU - 1, V, lower)
            weigh_values(NU - 3)
            project(NU - 1, V, upper)
            score(NU - 2, 2)
            square_sum(NU - 3)
            turn_probs(NU - 2, 0)
            turn_values(NU - 2)
            embed(0)
            embed(1)
            turn_probs(NU - 2, 1)
            embed(2)
            embed(3)
            turn_probs(NU - 2, 2)
            score(NU - 1, 0)
            spread_rms(NU - 3)
            embed(4)
            embed(5)
            weigh_values(NU - 2)
            score(NU - 1, 1)
            embed(6)
            turn_probs(NU - 1, 0)
            square_sum(NU - 2)
            embed(7)
            turn_values(NU - 1)
            score(NU - 1, 2)
            mix_out(0, range(0, 2))
            mix_out(0, range(2, 4))
            turn_probs(NU - 1, 1)
            spread_rms(NU - 2)
            mix_out(1, range(0, 2))
            mix_out(1, range(2, 4))
            turn_probs(NU - 1, 2)
            mix_out(0, range(4, 6))
            mix_out(1, range(4, 6))
            weigh_values(NU - 1)
            mix_out(2, range(0, 3))
            square_sum(NU - 1)
            mix_out(2, range(3, 6))
            mix_out(3, range(0, 3))
            spread_rms(NU - 1)
            mix_out(3, range(3, 6))
            for i in range(4):
                mix_out(i, range(6, 7))
            for i in range(4):
                mix_out(i, range(7, 8))
            for i in range(4, len(ITEMS)):
                if ITEMS[i][0] == "out":
                    mix_out(i, range(KT))
                elif ITEMS[i][0] == "turn":
                    turn_h(i)
                else:
                    gate(i)

        @block.scalar
        def _(act):
            A = nc.scalar.activation

            def weights_hi(j):
                act.wait_ge(raw_in[j % RAW], 16 * (j // RAW + (j % RAW > 1)))
                if 4 <= j < T_OUT:
                    act.wait_ge(proj, j - 3)
                elif j >= T_GATE + KT // 2:
                    act.wait_ge(item, 1 + number("out", 1, 3))
                elif j >= T_GATE:
                    act.wait_ge(pv, NU)
                elif j >= T_OUT + KT // 2:
                    act.wait_ge(pe_mm, ST * NH)
                elif j >= T_OUT:
                    act.wait_ge(proj, 4 * NU)
                hi = split_target(j)[0]
                if j < T_GATE:
                    A(hi, raw[:, j % RAW, :], ACT.Copy).then_inc(w_hi, 1)
                else:
                    for k in range(2):
                        kt = 2 * ((j - T_GATE) % (KT // 2)) + k
                        last = A(hi[:, k * SEQ:(k + 1) * SEQ], raw[:, j % RAW, k * SEQ:(k + 1) * SEQ], ACT.Copy, scale=gp[:, kt:kt + 1])
                    last.then_inc(w_hi, 1)

            def exponentials(u, step):
                act.wait_ge(maxes, 3 * u + step + 1)
                if u:
                    act.wait_ge(ptrans, 3 * u + step - 2)
                c = 0
                for q in STEP_TILES[step]:
                    n = (q + 1) * P
                    for m in range(2):
                        last = A(probs[:, m, STEP_COL[step] + c:STEP_COL[step] + c + n], sc[:, m, c:c + n], ACT.Exp,
                                 bias=nmax[:, q, m:m + 1], accum_out=rsum[:, q, m:m + 1])
                    c += n
                last.then_inc(exps, 1)

            def probs_hi(u, step):
                act.wait_ge(ptrans, 3 * u + step + 1)
                if step == 0 and u:
                    act.wait_ge(pv, u)
                for src, dst in per_map(pt_views(pt_hi, step), u < MOBA_UNITS):
                    last = A(dst, src, ACT.Copy)
                last.then_inc(p_hi, 1)

            def qk_hi_of(u, t):
                act.wait_ge(roped, 2 * u + t + 1)
                if u:
                    act.wait_ge(stacked, 128 * u)
                A(qksplit[:, t, 0, :], rot[:, t, :], ACT.Copy, scale=(SCALE, 1.0)[t]).then_inc(qk_hi, 1)

            def values_hi(u):
                act.wait_ge(vtrans, u + 1)
                if u:
                    act.wait_ge(pv, u)
                if u < MOBA_UNITS:
                    dst = vsplit[:, :, :].rearrange("p k (m i d) -> p k m i d", m=2, i=2)[:, :, :, 0, :]
                    src = ou[:, 0, :].rearrange("p (k m d) -> p k m d", k=ST, m=2)
                else:
                    dst = vsplit[:, :, 0:P]
                    src = ou[:, 0, :].rearrange("p (k d) -> p k d", k=ST)
                A(dst, src, ACT.Copy).then_inc(v_hi, 1)

            def output_copy(u):
                act.wait_ge(pv, u + 1)
                if u < MOBA_UNITS:
                    if u:
                        act.wait_ge(o_read, u)
                    A(o_tmp[0:HALF, :], ou[HALF:P, 0, :], ACT.Copy)
                    A(o_tmp[HALF:P, :], ou[0:HALF, 1, :], ACT.Copy).then_inc(o_half, 1)
                else:
                    if u > MOBA_UNITS:
                        act.wait_ge(o_bc, u - MOBA_UNITS)
                    A(o_tmp[:, :], ou[:, 0, :], ACT.Square).then_inc(o_sq, 1)
                    act.wait_ge(y_lo, u)
                    A(o_sb[:, :], ou[:, 0, :], ACT.Copy).then_inc(o_half, 1)

            def output_mean(u):
                act.wait_ge(o_ms, u - MOBA_UNITS + 1)
                A(rms4[:, :], ou[:, 1, 0:ST], ACT.Copy, scale=1.0 / P, bias=EPS).then_inc(o_mean, 1)

            def z_gate(u):
                act.wait_ge(pj_read, 4 * u + Z + 1)
                if u:
                    act.wait_ge(z_done, u)
                A(ztanh, zbuf[:, u % 3, :], ACT.Tanh).then_inc(z_tanh, 1)

            def y_round(u):
                act.wait_ge(y_ready, u + 1)
                A(ysplit[:, 0, u, :], o_sb[:, :], ACT.Copy).then_inc(y_hi, 1)

            def embed_read(g):
                t, n = divmod(g, NH)
                act.wait_ge(pe_mm, g + 1)
                if g == 0:
                    act.wait_ge(qk_lo, NU)
                    act.wait_ge(pj_read, 4 * NU)
                A(pe[:, t, n * SEQ:(n + 1) * SEQ], pj[:, g % 2, :], ACT.Copy, scale=0.5).then_inc(pe_read, 1)

            def h_square(k):
                _, n, t = [x for x in ITEMS if x[0] == "out"][k]
                act.wait_ge(h_read, k + 1)
                if k:
                    act.wait_ge(h_sq, k)
                A(v_t[:, :], h[:, t, n * SEQ:(n + 1) * SEQ], ACT.Square, accum_out=ssq[:, t, n:n + 1]).then_inc(h_sq, 1)

            def h_turned_hi(k):
                i = [x for x in range(len(ITEMS)) if ITEMS[x][0] == "turn"][k]
                _, n, t = ITEMS[i]
                act.wait_ge(item, i + 1)
                A(usplit[:, 0, 4 * n:4 * n + 4, t * P:(t + 1) * P], banks[BANK[i]].rearrange("p (b c) -> p b c", b=4),
                  ACT.Copy).then_inc(ht_hi, 1)

            def gate_tanh(k):
                i, _, t, o, _ = gate_part(k)
                act.wait_ge(item, i + 1)
                if k == 0:
                    act.wait_ge(h_rstd, 1)
                    act.wait_ge(y_lo, NU)
                if k >= 2:
                    act.wait_ge(g_add, k - 1)
                A((o_sb, o_tmp)[k % 2][:, 0:o.shape[1]], o, ACT.Tanh, scale=hrs[:, t:t + 1]).then_inc(g_tanh, 1)

            def f_square(k):
                _, n, t, _, c = gate_part(k)
                s = n + (k == len(GATES) - 1)
                act.wait_ge(g_add, k + 1)
                act.wait_ge(f_sq, k) if k else act.wait_ge(h_sq, ST * NH)
                A(v_t[:, 0:c.stop - c.start], h[:, t, c], ACT.Square, accum_out=fsq[:, t, s:s + 1]).then_inc(f_sq, 1)

            def final_scale_low(t):
                act.wait_ge(f_rstd, t + 1)
                act.wait_ge(f_gain, t + 1)
                A(h[:, t, 0:SEQ], h[:, t, 0:SEQ], ACT.Copy, scale=frs[:, t:t + 1]).then_inc(f_low, 1)

            act.dma_start(gm[:, :], g_mix).then_inc(gm_in, 16)
            for kt in (0, 2):
                act.dma_start(xt_raw[:, kt, :], x_t[kt * P:(kt + 1) * P, :]).then_inc(xt_in[kt], 16)

            act.wait_ge(gm_in, 16)
            for kt in range(KT):
                if kt % 2 == 0:
                    w = slice(128 * kt, 128 * kt + 256)
                    act.wait_ge(w0_in[kt // 2], 16)
                    A(wsplit[:, 0:2, 0, w], raw[:, 0:2, w], ACT.Copy).then_inc(w0_hi, 1)
                act.wait_ge(xt_in[kt], 16)
                A(usplit[:, 0, kt, :], xt_raw[:, kt, :], ACT.Copy, scale=gm[:, kt:kt + 1]).then_inc(u_hi, 1)
            for kt in range(0, KT, 2):
                act.wait_ge(u_lo, kt + 1)
                A(xt_raw[:, kt, :], xt_raw[:, kt, :], ACT.Square).then_inc(x_sq, 1)
            weights_hi(2)
            weights_hi(3)
            act.wait_ge(x_ms, 1)
            A(rms4[:, :], ou[:, 1, 0:ST], ACT.Copy, scale=1.0 / D_MODEL, bias=EPS).then_inc(x_mean, 1)
            act.wait_ge(lam_sum, 1)
            A(lam_e[:, :], lam_s[:, :], ACT.Exp).then_inc(lam_exp, 1)
            weights_hi(4)
            act.wait_ge(x_bc, 1)
            A(rstd, ou[:, 1, :], ACT.Copy).then_inc(rstd_done, 1)

            for u in range(NU - 1):
                if u >= 2:
                    probs_hi(u - 2, 1)
                if u:
                    weights_hi(4 * u + 3)
                if u >= 2:
                    probs_hi(u - 2, 2)
                if u:
                    weights_hi(4 * u + 4)
                if u >= 1:
                    exponentials(u - 1, 0)
                if u >= 3:
                    y_round(u - 3)
                if u >= 1:
                    exponentials(u - 1, 1)
                if u >= 2:
                    output_copy(u - 2)
                weights_hi(4 * u + 5)
                z_gate(u)
                qk_hi_of(u, Q)
                if u >= 1:
                    values_hi(u - 1)
                qk_hi_of(u, K)
                if u >= 1:
                    probs_hi(u - 1, 0)
                    exponentials(u - 1, 2)
                if u - 2 >= MOBA_UNITS:
                    output_mean(u - 2)
                weights_hi(4 * u + 6)
            probs_hi(NU - 3, 1)
            weights_hi(T_PLE - 1)
            probs_hi(NU - 3, 2)
            weights_hi(T_PLE)
            exponentials(NU - 2, 0)
            qk_hi_of(NU - 1, Q)
            weights_hi(T_PLE + 1)
            exponentials(NU - 2, 1)
            qk_hi_of(NU - 1, K)
            weights_hi(T_PLE + 2)
            y_round(NU - 4)
            output_copy(NU - 3)
            z_gate(NU - 1)
            probs_hi(NU - 2, 0)
            exponentials(NU - 2, 2)
            embed_read(0)
            values_hi(NU - 2)
            embed_read(1)
            output_mean(NU - 3)
            probs_hi(NU - 2, 1)
            weights_hi(T_OUT)
            embed_read(2)
            embed_read(3)
            probs_hi(NU - 2, 2)
            exponentials(NU - 1, 0)
            weights_hi(T_OUT + 1)
            y_round(NU - 3)
            embed_read(4)
            output_copy(NU - 2)
            embed_read(5)
            exponentials(NU - 1, 1)
            probs_hi(NU - 1, 0)
            embed_read(6)
            output_mean(NU - 2)
            embed_read(7)
            values_hi(NU - 1)
            weights_hi(T_OUT + 2)
            weights_hi(T_OUT + 3)
            exponentials(NU - 1, 2)
            probs_hi(NU - 1, 1)
            probs_hi(NU - 1, 2)
            weights_hi(T_OUT + 4)
            y_round(NU - 2)
            output_copy(NU - 1)
            output_mean(NU - 1)
            weights_hi(T_OUT + 5)
            y_round(NU - 1)
            for j in range(T_OUT + 6, T_GATE + KT // 2):
                weights_hi(j)
            for k in range(7):
                h_square(k)
            for k in (0, 1):
                h_turned_hi(k)
            h_square(7)
            for k in (2, 3):
                h_turned_hi(k)
            for j in range(T_GATE + KT // 2, T_ALL):
                weights_hi(j)
            gate_tanh(0)
            h_turned_hi(4), h_turned_hi(5)
            gate_tanh(1)
            h_turned_hi(6), h_turned_hi(7)
            for k in range(2, len(GATES)):
                f_square(k - 2)
                gate_tanh(k)
                if ST + 1 < k < 2 * ST:
                    final_scale_low(k - ST - 2)
            f_square(2 * ST - 1)
            final_scale_low(ST - 2)
            f_square(2 * ST)
            final_scale_low(ST - 1)

        @block.vector
        def _(dve):
            V_ = nc.vector

            def weights_lo(j):
                dve.wait_ge(w_hi, j - 1)
                hi, lo = split_target(j)
                if j < T_GATE:
                    V_.tensor_tensor(lo, raw[:, j % RAW, :], hi.bitcast(f32), ALU.subtract).then_inc(w_lo, 1)
                else:
                    for k in range(2):
                        kt, c = 2 * ((j - T_GATE) % (KT // 2)) + k, slice(k * SEQ, (k + 1) * SEQ)
                        last = V_.scalar_tensor_tensor(lo[:, c], raw[:, j % RAW, c], gp[:, kt:kt + 1], hi[:, c].bitcast(f32),
                                                       ALU.mult, ALU.subtract)
                    last.then_inc(w_lo, 1)

            def rope_start(u, t):
                n = 2 * u + t
                dve.wait_ge(proj, 4 * u + t + 1)
                if u:
                    dve.wait_ge(roped, n - 1)
                    dve.wait_ge(qk_lo, n - 1)
                o = pj_bank(4 * u + t)
                V_.stream_shuffle(shuf[:, t, :], o, [*range(8, 16), *range(8), *range(16, 32)])
                V_.tensor_tensor(rot[:, t, :], o, rope_r[:, 0, :], ALU.mult).then_inc(pj_read, 1)

            def z_scale(u):
                dve.wait_ge(proj, 4 * u + Z + 1)
                if u >= 3:
                    dve.wait_ge(y_ready, u - 2)
                V_.scalar_tensor_tensor(zbuf[:, u % 3, :], pj_bank(4 * u + Z), 0.5, rstd, ALU.mult, ALU.mult).then_inc(pj_read, 1)

            def z_silu(u):
                dve.wait_ge(z_tanh, u + 1)
                V_.scalar_tensor_tensor(zbuf[:, u % 3, :], ztanh, 1.0, zbuf[:, u % 3, :], ALU.add, ALU.mult).then_inc(z_done, 1)

            def v_scale(u):
                dve.wait_ge(proj, 4 * u + V + 1)
                if u:
                    dve.wait_ge(vtrans, u)
                V_.tensor_tensor(v_t[:, :], pj_bank(4 * u + V), rstd, ALU.mult).then_inc(pj_read, 1)

            def maxima(u, step):
                n = 3 * u + step
                dve.wait_ge(scores, n + 1)
                d = sc[:, :, 0:SEQ].rearrange("p m (b c) -> p m b c", c=P)
                if step == 0:
                    for m in range(2):
                        last = V_.tensor_tensor(d[:, m, 0:3:2, :], d[:, m, 0:3:2, :], mask.unsqueeze(1).broadcast_to([P, 2, P]), ALU.add)
                    last.then_inc(masked, 1)
                else:
                    b = STEP_W[step] // P - 1
                    V_.tensor_tensor(d[:, :, b, :], d[:, :, b, :], mask.unsqueeze(1).broadcast_to([P, 2, P]), ALU.add).then_inc(masked, 1)
                dve.wait_ge(masked, n + 1)
                c = 0
                for q in STEP_TILES[step]:
                    last = V_.tensor_reduce(nmax[:, q, :], sc[:, :, c:c + (q + 1) * P], AX.X, ALU.max, negate=True)
                    c += (q + 1) * P
                last.then_inc(maxes, 1)

            def reciprocals(u, step):
                n, tiles = 3 * u + step, slice(STEP_TILES[step][0], STEP_TILES[step][-1] + 1)
                dve.wait_ge(exps, n + 1)
                if u:
                    dve.wait_ge(probs_ready, n - 2)
                V_.reciprocal(rinv[:, tiles, :], rsum[:, tiles, :]).then_inc(recips, 1)
                if u >= MOBA_UNITS:
                    k = n - STEPS * MOBA_UNITS
                    if k == 0:
                        dve.wait_ge(lam_done, 1)
                    dve.wait_ge(recips, n + 1 + k)
                    V_.tensor_scalar(rinv[:, tiles, 1:2], rinv[:, tiles, 1:2], nlam[:, 0:1], None, ALU.mult).then_inc(recips, 1)

            def combine(u, step):
                n = 3 * u + step
                dve.wait_ge(weighted, n - STEPS * MOBA_UNITS + 1)
                c = STEP_COL[step]
                for q in STEP_TILES[step]:
                    w = slice(c, c + (q + 1) * P)
                    last = V_.scalar_tensor_tensor(probs[:, 0, w], probs[:, 0, w], rinv[:, q, 0:1], probs[:, 1, w], ALU.mult, ALU.add)
                    c += (q + 1) * P
                last.then_inc(probs_ready, 1)

            def probs_lo(u, step):
                dve.wait_ge(p_hi, 3 * u + step + 1)
                moba = u < MOBA_UNITS
                for (src, dst), (_, hi) in zip(per_map(pt_views(pt_lo, step), moba), per_map(pt_views(pt_hi, step), moba)):
                    last = V_.tensor_tensor(dst, src, hi.bitcast(f32), ALU.subtract)
                last.then_inc(p_lo, 1)

            def qk_lo_of(u, t):
                dve.wait_ge(qk_hi, 2 * u + t + 1)
                V_.scalar_tensor_tensor(qksplit[:, t, 1, :], rot[:, t, :], (SCALE, 1.0)[t], qksplit[:, t, 0, :].bitcast(f32),
                                        ALU.mult, ALU.subtract).then_inc(qk_lo, 1)

            def values_lo(u):
                dve.wait_ge(v_hi, u + 1)
                if u < MOBA_UNITS:
                    v = vsplit[:, :, :].rearrange("p k (m i d) -> p k m i d", m=2, i=2)
                    src = ou[:, 0, :].rearrange("p (k m d) -> p k m d", k=ST, m=2)
                    for m in range(2):
                        last = V_.tensor_tensor(v[:, :, m, 1, :], src[:, :, m, :], v[:, :, m, 0, :].bitcast(f32), ALU.subtract)
                    last.then_inc(v_lo, 1)
                else:
                    src = ou[:, 0, :].rearrange("p (k d) -> p k d", k=ST)
                    V_.tensor_tensor(vsplit[:, :, P:2 * P], src, vsplit[:, :, 0:P].bitcast(f32), ALU.subtract).then_inc(v_lo, 1)

            def output_sum(u):
                dve.wait_ge(o_half, u + 1)
                if u:
                    dve.wait_ge(y_lo, u)
                V_.tensor_tensor(o_sb[0:HALF, :], ou[0:HALF, 0, :], o_tmp[0:HALF, :], ALU.add)
                V_.tensor_tensor(o_sb[HALF:P, :], ou[HALF:P, 1, :], o_tmp[HALF:P, :], ALU.add).then_inc(o_read, 1)

            def output_norm(u):
                k = u - MOBA_UNITS
                dve.wait_ge(o_bc, k + 1)
                if k == 0:
                    dve.wait_ge(gs_done, 1)
                dve.wait_ge(o_half, u + 1)
                V_.scalar_tensor_tensor(o_sb[:, :], o_sb[:, :], gs8[:, 0:1], ou[:, 1, :], ALU.mult, ALU.mult).then_inc(o_read, 1)

            def widen_rms(u):
                dve.wait_ge(o_rstd, u - MOBA_UNITS + 1)
                V_.tensor_copy(o_tmp[:, :].rearrange("p (t c) -> p t c", t=ST),
                               rms4[:, :].unsqueeze(2).broadcast_to([P, ST, P])).then_inc(o_wide, 1)

            def y_rest(u):
                dve.wait_ge(y_hi, u + 1)
                V_.tensor_tensor(ysplit[:, 1, u, :], o_sb[:, :], ysplit[:, 0, u, :].bitcast(f32), ALU.subtract).then_inc(y_lo, 1)

            def residual(k):
                i = [x for x in range(len(ITEMS)) if ITEMS[x][0] == "out"][k]
                _, n, t = ITEMS[i]
                dve.wait_ge(item, i + 1)
                if n == 0:
                    dve.wait_ge(x_in[t], 16)
                c = slice(n * SEQ, (n + 1) * SEQ)
                V_.tensor_tensor(h[:, t, c], banks[BANK[i]], h[:, t, c], ALU.add).then_inc(h_read, 1)

            def h_turned_lo(k):
                i = [x for x in range(len(ITEMS)) if ITEMS[x][0] == "turn"][k]
                _, n, t = ITEMS[i]
                dve.wait_ge(ht_hi, k + 1)
                a = (slice(None), slice(4 * n, 4 * n + 4), slice(t * P, (t + 1) * P))
                V_.tensor_tensor(usplit[:, 1, a[1], a[2]], banks[BANK[i]].rearrange("p (b c) -> p b c", b=4),
                                 usplit[:, 0, a[1], a[2]].bitcast(f32), ALU.subtract).then_inc(ht_lo, 1)

            def gate_add(k):
                _, _, t, o, c = gate_part(k)
                g = (o_sb, o_tmp)[k % 2][:, 0:o.shape[1]]
                dve.wait_ge(g_tanh, k + 1)
                V_.scalar_tensor_tensor(g, g, 1.0, pe[:, t, c], ALU.add, ALU.mult).then_inc(g_mul, 1)
                dve.wait_ge(g_mul, k + 1)
                V_.tensor_tensor(h[:, t, c], h[:, t, c], g, ALU.add).then_inc(g_add, 1)

            def final_gain(k):
                _, _, t, _, c = gate_part(k)
                dve.wait_ge(f_sq, k + 1)
                V_.tensor_tensor(h[:, t, c], h[:, t, c], gfin[:, c], ALU.mult).then_inc(f_gain, 1)

            def final_scale(t):
                dve.wait_ge(f_rstd, t + 1)
                dve.wait_ge(f_gain, ST + t + 1 + (t == ST - 1))
                V_.tensor_scalar(h[:, t, SEQ:], h[:, t, SEQ:], frs[:, t:t + 1], None, ALU.mult).then_inc(f_high, 1)

            for kt in range(KT):
                if kt % 2 == 0:
                    w = slice(128 * kt, 128 * kt + 256)
                    dve.wait_ge(w0_hi, kt // 2 + 1)
                    V_.tensor_tensor(wsplit[:, 0:2, 1, w], raw[:, 0:2, w], wsplit[:, 0:2, 0, w].bitcast(f32), ALU.subtract).then_inc(w0_lo, 1)
                dve.wait_ge(u_hi, kt + 1)
                V_.scalar_tensor_tensor(usplit[:, 1, kt, :], xt_raw[:, kt, :], gm[:, kt:kt + 1], usplit[:, 0, kt, :].bitcast(f32),
                                        ALU.mult, ALU.subtract).then_inc(u_lo, 1)
            for kt in range(1, KT):
                dve.wait_ge(x_sq, kt // 2 + 1)
                dve.wait_ge(pool_own, (kt + 1) // 2)
                if kt > 1:
                    dve.wait_ge(x_sum, kt - 1)
                a = xt_raw[:, 0, :] if kt == 1 else xsum[:, :]
                V_.tensor_tensor(xsum[:, :], a, xt_raw[:, kt, :], ALU.add).then_inc(x_sum, 1)
            weights_lo(2)
            weights_lo(3)
            dve.wait_ge(small_in, 64)
            V_.tensor_tensor(lam_pr[:, :, :], lam_in[:, 0:3:2, :], lam_in[:, 1:4:2, :], ALU.mult).then_inc(lam_prod, 1)
            dve.wait_ge(lam_prod, 1)
            V_.tensor_reduce(lam_s[:, :], lam_pr[:, :, :], AX.X, ALU.add).then_inc(lam_sum, 1)
            V_.tensor_scalar(gs8[:, :], gs[:, :], 1.0 - LAMBDA_INIT, None, ALU.mult).then_inc(gs_done, 1)
            dve.wait_ge(x_rstd, 1)
            V_.tensor_copy(xsum[:, :].rearrange("p (t c) -> p t c", t=ST),
                           rms4[:, :].unsqueeze(2).broadcast_to([P, ST, P])).then_inc(x_wide, 1)
            dve.wait_ge(lam_exp, 1)
            V_.tensor_scalar(nlam[:, :], lam_e[:, 1:2], lam_e[:, 0:1], LAMBDA_INIT, ALU.subtract, ALU.subtract).then_inc(lam_done, 1)
            weights_lo(4)
            dve.wait_ge(rstd_done, 1)
            dve.wait_ge(rope_in, 16)
            for i in range(2):
                last = V_.tensor_tensor(rope_r[:, i, :], rope_r[:, i, :], rstd, ALU.mult)
            last.then_inc(tab_done, 1)
            dve.wait_ge(tab_done, 1)

            def inverses(u, step):
                reciprocals(u, step)
                if u >= MOBA_UNITS:
                    combine(u, step)

            for u in range(NU - 1):
                if u >= 2:
                    probs_lo(u - 2, 1)
                rope_start(u, Q)
                if u:
                    weights_lo(4 * u + 3)
                rope_start(u, K)
                if u >= 1:
                    maxima(u - 1, 0)
                    inverses(u - 1, 0)
                if u >= 2:
                    probs_lo(u - 2, 2)
                if u - 3 >= MOBA_UNITS:
                    output_norm(u - 3)
                z_scale(u)
                if u - 3 >= MOBA_UNITS:
                    widen_rms(u - 3)
                if u:
                    weights_lo(4 * u + 4)
                if u >= 1:
                    maxima(u - 1, 1)
                if u >= 3:
                    y_rest(u - 3)
                if u >= 1:
                    inverses(u - 1, 1)
                if 0 <= u - 2 < MOBA_UNITS:
                    output_sum(u - 2)
                if u >= 1:
                    maxima(u - 1, 2)
                z_silu(u)
                qk_lo_of(u, Q)
                qk_lo_of(u, K)
                weights_lo(4 * u + 5)
                if u >= 1:
                    probs_lo(u - 1, 0)
                v_scale(u)
                if u >= 1:
                    values_lo(u - 1)
                    inverses(u - 1, 2)
                weights_lo(4 * u + 6)
            probs_lo(NU - 3, 1)
            weights_lo(T_PLE - 1)
            widen_rms(NU - 4)
            rope_start(NU - 1, Q)
            rope_start(NU - 1, K)
            maxima(NU - 2, 0)
            probs_lo(NU - 3, 2)
            output_norm(NU - 4)
            inverses(NU - 2, 0)
            qk_lo_of(NU - 1, Q)
            maxima(NU - 2, 1)
            weights_lo(T_PLE)
            weights_lo(T_PLE + 1)
            z_scale(NU - 1)
            inverses(NU - 2, 1)
            weights_lo(T_PLE + 2)
            qk_lo_of(NU - 1, K)
            y_rest(NU - 4)
            maxima(NU - 2, 2)
            v_scale(NU - 1)
            probs_lo(NU - 2, 0)
            inverses(NU - 2, 2)
            values_lo(NU - 2)
            probs_lo(NU - 2, 1)
            widen_rms(NU - 3)
            z_silu(NU - 1)
            weights_lo(T_OUT)
            maxima(NU - 1, 0)
            output_norm(NU - 3)
            probs_lo(NU - 2, 2)
            inverses(NU - 1, 0)
            y_rest(NU - 3)
            maxima(NU - 1, 1)
            weights_lo(T_OUT + 1)
            inverses(NU - 1, 1)
            probs_lo(NU - 1, 0)
            values_lo(NU - 1)
            maxima(NU - 1, 2)
            widen_rms(NU - 2)
            weights_lo(T_OUT + 2)
            inverses(NU - 1, 2)
            probs_lo(NU - 1, 1)
            output_norm(NU - 2)
            probs_lo(NU - 1, 2)
            weights_lo(T_OUT + 3)
            y_rest(NU - 2)
            widen_rms(NU - 1)
            output_norm(NU - 1)
            weights_lo(T_OUT + 4)
            weights_lo(T_OUT + 5)
            y_rest(NU - 1)
            for j in range(T_OUT + 6, T_GATE):
                weights_lo(j)
            for k in range(4):
                residual(k)
            for j in range(T_GATE, T_GATE + KT // 2):
                weights_lo(j)
            for k in range(4, 7):
                residual(k)
            h_turned_lo(0), h_turned_lo(1)
            residual(7)
            h_turned_lo(2), h_turned_lo(3)
            for j in range(T_GATE + KT // 2, T_ALL):
                weights_lo(j)
            h_turned_lo(4), h_turned_lo(5)
            gate_add(0)
            h_turned_lo(6), h_turned_lo(7)
            for k in range(1, len(GATES)):
                gate_add(k)
                final_gain(k - 1)
                if ST < k < 2 * ST:
                    final_scale(k - ST - 1)
            final_gain(2 * ST)
            final_scale(ST - 1)

        @block.gpsimd
        def _(pool):
            G = nc.gpsimd
            own = [0]

            def link(ins):
                own[0] += 1
                ins.then_inc(pool_own, 1)
                pool.wait_ge(pool_own, own[0])

            def rope_finish(u, t):
                pool.wait_ge(pj_read, 4 * u + t + 1)
                pool.wait_ge(tab_done, 1)
                link(G.tensor_tensor(shuf[:, t, :], shuf[:, t, :], rope_r[:, 1, :], ALU.mult))
                G.tensor_tensor(rot[:, t, :], rot[:, t, :], shuf[:, t, :], ALU.add).then_inc(roped, 1)

            def normalise(u, step):
                n = 3 * u + step
                moba = u < MOBA_UNITS
                pool.wait_ge(recips, n + 1 if moba else 2 * n + 2 - STEPS * MOBA_UNITS)
                c = STEP_COL[step]
                for q in STEP_TILES[step]:
                    w = slice(c, c + (q + 1) * P)
                    for m in (0, 1) if moba else (1,):
                        last = G.tensor_scalar(probs[:, m, w], probs[:, m, w], rinv[:, q, m:m + 1], 1.0, ALU.mult, ALU.mult)
                    c += (q + 1) * P
                last.then_inc(probs_ready if moba else weighted, 1)

            def gate_output(u):
                pool.wait_ge(o_read, u + 1)
                pool.wait_ge(z_done, u + 1)
                G.tensor_tensor(o_sb[:, :], o_sb[:, :], zbuf[:, u % 3, :], ALU.mult).then_inc(y_ready, 1)

            for kt in range(1, KT, 2):
                pool.wait_ge(u_lo, kt + 1)
                own[0] += 1
                G.tensor_tensor(xt_raw[:, kt, :], xt_raw[:, kt, :], xt_raw[:, kt, :], ALU.mult).then_inc(pool_own, 1)
            link(G.memset(mhalf[:, :], -0.5))

            def token_rms(mean_done, count, done):
                pool.wait_ge(mean_done, count)
                G.tensor_tensor(rms4[:, :], rms4[:, :], mhalf[:, :], ALU.pow).then_inc(done, 1)

            token_rms(x_mean, 1, x_rstd)
            for u in range(NU):
                if u - 3 >= MOBA_UNITS:
                    token_rms(o_mean, u - 3 - MOBA_UNITS + 1, o_rstd)
                rope_finish(u, Q)
                rope_finish(u, K)
                if u:
                    normalise(u - 1, 0)
                if u >= 3:
                    gate_output(u - 3)
                if u:
                    normalise(u - 1, 1)
                    normalise(u - 1, 2)
            token_rms(o_mean, NU - MOBA_UNITS - 2, o_rstd)
            gate_output(NU - 3)
            normalise(NU - 1, 0)
            normalise(NU - 1, 1)
            token_rms(o_mean, NU - MOBA_UNITS - 1, o_rstd)
            normalise(NU - 1, 2)
            gate_output(NU - 2)
            token_rms(o_mean, NU - MOBA_UNITS, o_rstd)
            gate_output(NU - 1)
            pool.wait_ge(h_sq, ST * NH)
            link(G.tensor_tensor(ssa[:, :], ssq[:, :, 0], ssq[:, :, 1], ALU.add))
            link(G.tensor_scalar(ssa[:, :], ssa[:, :], 1.0 / D_MODEL, EPS, ALU.mult, ALU.add))
            link(G.tensor_tensor(ssa[:, :], ssa[:, :], mhalf[:, :], ALU.pow))
            G.tensor_scalar(hrs[:, :], ssa[:, :], 0.5, 1.0, ALU.mult, ALU.mult).then_inc(h_rstd, 1)
            pool.wait_ge(f_sq, ST)
            link(G.tensor_scalar(fsa[:, :], fsq[:, :, 0], 1.0 / D_MODEL, EPS, ALU.mult, ALU.add))
            for t in range(ST):
                pool.wait_ge(f_sq, ST + t + 1)
                link(G.tensor_scalar(fsa[:, t:t + 1], fsq[:, t, 1:2], 1.0 / D_MODEL, fsa[:, t:t + 1], ALU.mult, ALU.add))
                if t == ST - 1:
                    pool.wait_ge(f_sq, len(GATES))
                    link(G.tensor_scalar(fsa[:, t:t + 1], fsq[:, t, 2:3], 1.0 / D_MODEL, fsa[:, t:t + 1], ALU.mult, ALU.add))
                G.tensor_tensor(frs[:, t:t + 1], fsa[:, t:t + 1], mhalf[:, 0:1], ALU.pow).then_inc(f_rstd, 1)


def kernel(**inputs):
    import concourse.bacc as bacc
    from concourse.bass_utils import run_bass_kernel_spmd as run

    a = {k: np.asarray(v) for k, v in inputs.items()}
    units = D_MODEL // P
    starts = []
    for u in range(units):
        part, q = (0, u) if u < units // 2 else (3, u - units // 2)
        starts += [(part + i) * 512 + q * P for i in (0, 1)] + [3072 + u * P, (part + 2) * 512 + q * P]
    w = a["w_in"][0].reshape(D_MODEL // P, P, -1)
    w_in = np.stack([w[:, :, c:c + P] for c in starts])
    w_in = w_in.reshape(units, 4, D_MODEL // P, P, P).transpose(0, 3, 1, 2, 4)

    inv = np.float32(ROPE_THETA) ** (-np.arange(0, ROPE_DIM, 2, dtype=np.float32) / np.float32(ROPE_DIM))
    ang = inv[:, None] * np.arange(SEQ, dtype=np.float32)[None, :]
    rope = np.zeros((2, P, SEQ), np.float32)
    rope[0] = 1.0
    for b in range(0, P, HEAD_DIM):
        rope[0, b:b + ROPE_DIM] = np.tile(np.cos(ang), (2, 1))
        rope[1, b:b + ROPE_DIM] = np.concatenate([-np.sin(ang), np.sin(ang)])
    consts = np.concatenate([np.eye(P), np.where(np.tri(P) > 0, 0.0, -3e38), np.ones((P, P))], 1).astype(np.float32)

    arrays = {
        "x_t": a["x"][0].T, "x": a["x"][0], "p_t": a["p"][0, 0].T,
        "w_in": w_in.reshape(units, P, 4, D_MODEL), "w_out": a["w_out"][0], "w_gate": a["w_ple_gate"][0], "w_ple": a["w_ple"][0],
        "g_mix": a["g_mix"][0].reshape(-1, P).T, "g_ple": a["g_ple"][0].reshape(-1, P).T,
        "g_subln": a["g_subln"][0].reshape(P, 1), "g_final": a["g_final"],
        "lams": np.stack([a[n][0] for n in ("diff_lq1", "diff_lk1", "diff_lq2", "diff_lk2")]),
        "rope": rope, "consts": consts,
    }
    arrays = {f"in_{k}": np.ascontiguousarray(v) for k, v in arrays.items()}
    nc = bacc.Bacc("TRN2", target_bir_lowering=False, num_devices=1)
    args = [nc.dram_tensor(k, v.shape, mybir.dt.from_np(v.dtype), kind="ExternalInput").ap() for k, v in arrays.items()]
    out = nc.dram_tensor("out", (SEQ, D_MODEL), mybir.dt.float32, kind="ExternalOutput").ap()
    build_program(nc, *args, out)
    r = run(nc, [arrays], core_ids=[0])
    return r.results[0]["out"].reshape(1, SEQ, D_MODEL)
```
